# Optimizing a Trainium2 kernel written in Bass

```python
import jax, jax.numpy as jnp
from jax import lax
import numpy as np

D_MODEL = 1024
BATCH = 1
SEQ = 256
DEPTH = 2
DEC_BATCH = 8
DEC_SEQ = 1
PAST_LEN = 2048
PAGE_SIZE = 128

LRU_WIDTH = D_MODEL
LRU_HEADS = 16
LRU_BLOCK = LRU_WIDTH // LRU_HEADS
CONV_A_WIDTH = 4
LRU_C = 8.0
SC_WIDTH = D_MODEL
CONV_B_WIDTH = 3
PLE_DIM = 256
D_FF = 3 * D_MODEL
N_EXPERTS = 8
TOP_K = 2
D_FF_EXPERT = 3 * D_MODEL // 2
N_DENSE = (DEPTH + 1) // 2
N_MOE = DEPTH // 2
EPS = 1e-6
IN_COLS = 2 * LRU_WIDTH + 3 * SC_WIDTH + 2 * D_MODEL
SPLIT_IDX = (LRU_WIDTH, 2 * LRU_WIDTH, 2 * LRU_WIDTH + SC_WIDTH,
             2 * LRU_WIDTH + 2 * SC_WIDTH, 2 * LRU_WIDTH + 3 * SC_WIDTH,
             2 * LRU_WIDTH + 3 * SC_WIDTH + D_MODEL)

kernel_name = "hawk_shortconv_parallel_hybrid_step"

def rms_norm(x, g):
    xf = x.astype(jnp.float32)
    var = jnp.mean(xf * xf, axis=-1, keepdims=True)
    return (xf * lax.rsqrt(var + EPS) * g.astype(jnp.float32)).astype(x.dtype)

def causal_dwconv(x, buf, w):
    k = w.shape[0]
    t = x.shape[1]
    xp = jnp.concatenate([buf.astype(x.dtype), x], axis=1)
    y = xp[:, 0:t] * w[0]
    for j in range(1, k):
        y = y + xp[:, j:j + t] * w[j]
    return y, xp[:, t:]

def rg_lru(x, wx, bx, wa, ba, lam, h0):
    b_, t, w = x.shape
    xh = x.reshape(b_, t, LRU_HEADS, LRU_BLOCK)
    gate_x = jax.nn.sigmoid((jnp.einsum('bthi,hij->bthj', xh, wx).reshape(b_, t, w) + bx).astype(jnp.float32))
    gate_a = jax.nn.sigmoid((jnp.einsum('bthi,hij->bthj', xh, wa).reshape(b_, t, w) + ba).astype(jnp.float32))
    log_a = LRU_C * gate_a * jax.nn.log_sigmoid(lam.astype(jnp.float32))
    a = jnp.exp(log_a)
    mult = jnp.sqrt(-jnp.expm1(2.0 * log_a))
    b = mult * gate_x * x.astype(jnp.float32)
    b = b.at[:, 0].add(a[:, 0] * h0.astype(jnp.float32))

    def combine(left, right):
        al, bl = left
        ar, br = right
        return al * ar, ar * bl + br

    _, h = lax.associative_scan(combine, (a, b), axis=1)
    return h.astype(x.dtype), h[:, -1]

def swiglu(x, w_gu, w_dn):
    g, u = jnp.split(x @ w_gu, 2, axis=-1)
    return (jax.nn.silu(g) * u) @ w_dn

def moe_swiglu(x, router, w_gu, w_dn):
    logits = jnp.einsum('btd,de->bte', x, router).astype(jnp.float32)
    top_v, top_i = lax.top_k(logits, TOP_K)
    top_w = jax.nn.softmax(top_v, axis=-1)
    comb = jnp.einsum('btk,btke->bte', top_w,
                      jax.nn.one_hot(top_i, N_EXPERTS, dtype=jnp.float32)).astype(x.dtype)
    out = jnp.zeros_like(x)
    for e in range(N_EXPERTS):
        out = out + comb[..., e:e + 1] * swiglu(x, w_gu[e], w_dn[e])
    return out

def setup_inputs(seed: int = 0) -> dict:
    key = jax.random.key(seed)
    ks = iter(jax.random.split(key, 40))
    f32 = jnp.float32

    def nrm(shape, scale):
        return jax.random.normal(next(ks), shape, f32) * scale

    def gain(shape):
        return 1.0 + 0.05 * jax.random.normal(next(ks), shape, f32)

    out_scale = (2.0 * DEPTH) ** -0.5
    a0 = jax.random.uniform(next(ks), (DEPTH, LRU_WIDTH), f32, 0.9, 0.999)
    s = a0 ** (1.0 / LRU_C)
    lru_lambda = jnp.log(s) - jnp.log1p(-s)
    return {
        "x_prompt": nrm((BATCH, SEQ, D_MODEL), 1.0),
        "x_sample": nrm((DEC_BATCH, DEC_SEQ, D_MODEL), 1.0),
        "state_lru_h": nrm((DEPTH, DEC_BATCH, LRU_WIDTH), 0.5),
        "state_conv_a": nrm((DEPTH, DEC_BATCH, CONV_A_WIDTH - 1, LRU_WIDTH), 1.0),
        "state_conv_b": nrm((DEPTH, DEC_BATCH, CONV_B_WIDTH - 1, SC_WIDTH), 1.0),
        "p_prompt": nrm((DEPTH, BATCH, SEQ, PLE_DIM), 1.0),
        "p_sample": nrm((DEPTH, DEC_BATCH, DEC_SEQ, PLE_DIM), 1.0),
        "norm_mix": gain((DEPTH, D_MODEL)),
        "w_in": nrm((DEPTH, D_MODEL, IN_COLS), D_MODEL ** -0.5),
        "conv_a_w": nrm((DEPTH, CONV_A_WIDTH, LRU_WIDTH), CONV_A_WIDTH ** -0.5),
        "conv_a_b": nrm((DEPTH, LRU_WIDTH), 0.02),
        "lru_wx": nrm((DEPTH, LRU_HEADS, LRU_BLOCK, LRU_BLOCK), LRU_BLOCK ** -0.5),
        "lru_bx": nrm((DEPTH, LRU_WIDTH), 0.02),
        "lru_wa": nrm((DEPTH, LRU_HEADS, LRU_BLOCK, LRU_BLOCK), LRU_BLOCK ** -0.5),
        "lru_ba": nrm((DEPTH, LRU_WIDTH), 0.02),
        "lru_lambda": lru_lambda,
        "w_a_out": nrm((DEPTH, LRU_WIDTH, D_MODEL), LRU_WIDTH ** -0.5),
        "conv_b_w": nrm((DEPTH, CONV_B_WIDTH, SC_WIDTH), CONV_B_WIDTH ** -0.5),
        "w_b_out": nrm((DEPTH, SC_WIDTH, D_MODEL), SC_WIDTH ** -0.5),
        "w_o": nrm((DEPTH, D_MODEL, D_MODEL), D_MODEL ** -0.5 * out_scale),
        "norm_ffn": gain((DEPTH, D_MODEL)),
        "ffn_w_gu": nrm((N_DENSE, D_MODEL, 2 * D_FF), D_MODEL ** -0.5),
        "ffn_w_dn": nrm((N_DENSE, D_FF, D_MODEL), D_FF ** -0.5 * out_scale),
        "router": nrm((N_MOE, D_MODEL, N_EXPERTS), D_MODEL ** -0.5),
        "moe_w_gu": nrm((N_MOE, N_EXPERTS, D_MODEL, 2 * D_FF_EXPERT), D_MODEL ** -0.5),
        "moe_w_dn": nrm((N_MOE, N_EXPERTS, D_FF_EXPERT, D_MODEL), D_FF_EXPERT ** -0.5 * out_scale),
        "norm_ple": gain((DEPTH, D_MODEL)),
        "w_ple_gate": nrm((DEPTH, D_MODEL, D_MODEL), D_MODEL ** -0.5),
        "w_ple_proj": nrm((DEPTH, PLE_DIM, D_MODEL), PLE_DIM ** -0.5 * out_scale),
        "final_norm": gain((D_MODEL,)),
    }

def reference(x_prompt, x_sample, state_lru_h, state_conv_a, state_conv_b, p_prompt, p_sample,
              norm_mix, w_in, conv_a_w, conv_a_b, lru_wx, lru_bx, lru_wa, lru_ba, lru_lambda,
              w_a_out, conv_b_w, w_b_out, w_o, norm_ffn, ffn_w_gu, ffn_w_dn, router,
              moe_w_gu, moe_w_dn, norm_ple, w_ple_gate, w_ple_proj, final_norm):

    def run(x, p, lru0, ca0, cb0):
        h = x
        lru_s, ca_s, cb_s = [], [], []
        for i in range(DEPTH):
            n = rms_norm(h, norm_mix[i])
            z = n @ w_in[i]
            xa, ya, xb, g_post, g_pre, m_a, m_b = jnp.split(z, SPLIT_IDX, axis=-1)
            ua, ca_new = causal_dwconv(xa, ca0[i], conv_a_w[i])
            ua = ua + conv_a_b[i]
            ha, h_last = rg_lru(ua, lru_wx[i], lru_bx[i], lru_wa[i], lru_ba[i], lru_lambda[i], lru0[i])
            out_a = (ha * jax.nn.gelu(ya)) @ w_a_out[i]
            ub, cb_new = causal_dwconv(g_pre * xb, cb0[i], conv_b_w[i])
            out_b = (g_post * ub) @ w_b_out[i]
            merged = jax.nn.sigmoid(m_a) * out_a + jax.nn.sigmoid(m_b) * out_b
            h = h + merged @ w_o[i]
            n2 = rms_norm(h, norm_ffn[i])
            if i % 2 == 0:
                h = h + swiglu(n2, ffn_w_gu[i // 2], ffn_w_dn[i // 2])
            else:
                h = h + moe_swiglu(n2, router[i // 2], moe_w_gu[i // 2], moe_w_dn[i // 2])
            e_i = p[i] @ w_ple_proj[i]
            h = h + jax.nn.sigmoid(rms_norm(h, norm_ple[i]) @ w_ple_gate[i]) * e_i
            lru_s.append(h_last.astype(lru0.dtype))
            ca_s.append(ca_new.astype(ca0.dtype))
            cb_s.append(cb_new.astype(cb0.dtype))
        return rms_norm(h, final_norm), jnp.stack(lru_s), jnp.stack(ca_s), jnp.stack(cb_s)

    dt = x_prompt.dtype
    lru0_p = jnp.zeros((DEPTH, x_prompt.shape[0], LRU_WIDTH), dt)
    ca0_p = jnp.zeros((DEPTH, x_prompt.shape[0], CONV_A_WIDTH - 1, LRU_WIDTH), dt)
    cb0_p = jnp.zeros((DEPTH, x_prompt.shape[0], CONV_B_WIDTH - 1, SC_WIDTH), dt)
    y_prompt, lru_p, ca_p, cb_p = run(x_prompt, p_prompt, lru0_p, ca0_p, cb0_p)
    y_sample, lru_d, ca_d, cb_d = run(x_sample, p_sample, state_lru_h, state_conv_a, state_conv_b)
    return (y_prompt, y_sample, lru_p, ca_p, cb_p, lru_d, ca_d, cb_d)


_drawn_inputs = setup_inputs


def setup_inputs(seed=0):
    import zlib

    import numpy as np

    out = dict(_drawn_inputs(seed))
    spreads = {}
    factors = {'lru_bx': 7.951, 'lru_ba': 8.0, 'norm_ple': 6.248}
    for name, (base, spread) in spreads.items():
        noise = np.random.default_rng([zlib.crc32(name.encode()), seed]).standard_normal(out[name].shape)
        drawn = base * np.exp(spread * noise) if base else spread * noise
        out[name] = __import__('jax').numpy.asarray(drawn.astype(out[name].dtype))
    for name, factor in factors.items():
        out[name] = (out[name] * factor).astype(out[name].dtype)
    return out
```

```python
import math
from contextlib import ExitStack

import concourse.bass as bass
from concourse import mybir

F32 = mybir.dt.float32
F16 = mybir.dt.float16
ALU = mybir.AluOpType
ACT = mybir.ActivationFunctionType
AX = mybir.AxisListType

P = 128
SEQ, NSAMP, D, LAYERS = 256, 8, 1024, 2
T = SEQ + NSAMP
C = D // P
HEADS, HB = 16, 64
PLE, PC = 256, 2
FF, FE, NE = 3072, 1536, 8
EPS = 1e-6

WS, XS = 256.0, 16.0
UNSCALE = 1.0 / (WS * XS)

SLOTS = 4
MOE_SLOTS = SLOTS + 1
UNIT = 2048
LEAD = SLOTS - 1

SEC = 4
FFN_IT, MOE_GU, MOE_DN = FF // 512, 2 * FE // 256, 8
EC = FE // P
DN_K = EC // 4
CAP = 96
SPILLS = -(-T // CAP) - 1
TOK = ((0, P), (P, P), (SEQ, NSAMP))
MOE_U = MOE_GU + MOE_DN

IN_SECTIONS = 7
MIX_U = (IN_SECTIONS + 3) * SEC
N_MIX = [0, MIX_U + (FFN_IT + 3) * SEC + SEC]
N_GU = N_MIX[0] + MIX_U
N_DN = N_GU + FFN_IT * SEC
N_MOE = N_MIX[1] + MIX_U
N_PLE = [N_DN + 3 * SEC, N_MOE + NE * MOE_U]
MOE_EVAC = MOE_GU + 2
UNCOUNTED = NE * (MOE_U - MOE_EVAC)
N_END = N_PLE[1] + SEC

IN_RUNS = [(1, 2, 1), (3, 1, 4), (4, 1, 3), (5, 2, 5)]

GELU_C = math.sqrt(2.0 / math.pi)
A_EXT = 3 + T + 24
B_EXT = 2 + T + 16


def row_table():
    at, out = 0, {}
    for name, n in (("norm_mix", 2), ("conv_a_w", 8), ("conv_a_b", 2), ("lru_bx", 2), ("lru_ba", 2),
                    ("lru_lambda", 2), ("conv_b_w", 6), ("norm_ffn", 2), ("norm_ple", 2), ("final_norm", 1),
                    ("state_lru_h", 16), ("state_conv_a", 48), ("state_conv_b", 32)):
        out[name] = (at, n)
        at += n
    return out, at


ROWS, N_ROWS = row_table()


def raw_turn(n):
    if n < N_MOE:
        return n % SLOTS, n // SLOTS + 1
    if n < N_PLE[1]:
        u = n - N_MOE
        return u % MOE_SLOTS, u // MOE_SLOTS + 1 + (N_MOE // SLOTS if u % MOE_SLOTS < SLOTS else 0)
    return (n - N_PLE[1]) % SLOTS, N_MOE // SLOTS + NE * MOE_U // MOE_SLOTS + 1


def moe_unit_size(u):
    return UNIT if u % MOE_U < MOE_GU else DN_K * 512


def program(nc, a, o):
    ctx = ExitStack()
    with ctx:
        def sb(name, shape, dt=F32):
            return ctx.enter_context(nc.sbuf_tensor(name, shape, dt))

        def sem(name):
            return ctx.enter_context(nc.semaphore(name))
        raw = sb("raw", [P, SLOTS, UNIT])
        wh = sb("wh", [P, SLOTS, UNIT], F16)
        wl = sb("wl", [P, SLOTS, UNIT], F16)
        h = sb("h", [P, C, T])
        xa = sb("xa", [P, C, A_EXT])
        ub = sb("ub", [P, C, B_EXT])
        ya = sb("ya", [P, C, T])
        xb = sb("xb", [P, C, T])
        sa = sb("sa", [P, C, T])
        sg = sb("sg", [P, C, T])
        w1 = sb("w1", [P, 3, C, T])
        xn = sb("xn", [P, 2, C, T], F16)
        ga = sb("ga", [P, 2, C, T], F16)
        gb = sb("gb", [P, 2, C, T], F16)
        side = sb("side", [P, 2, C, P])
        vec = sb("vec", [P, C, P])
        pt = sb("pt", [P, LAYERS, PC, T])
        ot = sb("ot", [P, 2, 2, T])
        var = sb("var", [P, T])
        std = sb("std", [P, T])
        rstd = sb("rstd", [P, T])
        rtmp = sb("rtmp", [P, T])
        ident = sb("ident", [P, P])
        ones = sb("ones", [P, P])
        tri = sb("tri", [P, NE, NE])
        eps = sb("eps", [P, 1])
        root = sb("root", [P, 1])
        tiny = sb("tiny", [P, 1])
        hb = sb("hb", [P, C, 4])
        sp4 = sb("sp4", [P, C, LAYERS])
        lam_a = sb("lam_a", [P, C, LAYERS])
        lam_b = sb("lam_b", [P, C, LAYERS])
        lam_c = sb("lam_c", [P, C, LAYERS])
        lam_d = sb("lam_d", [P, C, LAYERS])
        smp = sb("smp", [P, C, NSAMP])
        smq = sb("smq", [P, C, NSAMP])
        st = sb("st", [P, C, 30])
        rows = sb("rows", [32, D])
        rt = sb("rt", [P, C, NE])
        lg = sb("lg", [P, 3, NE])
        prs = sb("prs", [P, 3, NE + 1, 2], F16)
        prs_e = sb("prs_e", [P, 3, 2], F16)
        iota = sb("iota", [P, CAP])
        slot_id = sb("slot_id", [P, 1])
        pos = sb("pos", [P, 3, NE + 1])
        over = sb("over", [NE, 1])
        flag = sb("flag", [1, 1], mybir.dt.int32)
        spare = sb("spare", [1, 5])
        csr = sb("csr", [P, 2])
        csl = sb("csl", [P, 1])
        identh = sb("identh", [P, P], F16)
        cmp_a = sb("cmp_a", [P, NE, NE])
        cmp_b = sb("cmp_b", [P, NE, NE])
        rank = sb("rank", [P, 3, NE])
        top = sb("top", [P, 3])
        den = sb("den", [P, 3])
        pr = sb("pr", [P, 3, NE])

        nf = xb
        raw_slot = [raw[:, i] for i in range(SLOTS)] + [xb[:].rearrange("p c t -> p (c t)")[:, 0:UNIT]]
        sq = sa
        ua, gx, gy = w1[:, 0], w1[:, 1], w1[:, 2]
        ga_f = ga[:].rearrange("p a c t -> p (a c t)").bitcast(F32).rearrange("p (c t) -> p c t", c=C)
        gb_f = gb[:].rearrange("p a c t -> p (a c t)").bitcast(F32).rearrange("p (c t) -> p c t", c=C)
        hid = w1[:].rearrange("p a c t -> p (a c t)").bitcast(F16).rearrange("p (s c t) -> p s c t", s=2, c=24)
        w1_flat = w1[:].rearrange("p a c t -> p (a c t)")
        vrows = w1_flat[:, 0:D]
        xrows = w1_flat[:, D:D + 3 * D].rearrange("p (t n) -> p t n", t=3)
        prows = w1_flat[:, 4 * D:4 * D + 3 * LAYERS * PLE].rearrange("p (l t n) -> p l t n", l=LAYERS, t=3)
        yrows = w1_flat[:, 0:3 * D].rearrange("p (t n) -> p t n", t=3)
        w1_half = w1_flat.bitcast(F16)
        hid_e = w1_half[:, 0:2 * EC * CAP].rearrange("p (s c t) -> p s c t", s=2, c=EC)
        at = 2 * EC * CAP
        nt = w1_half[:, at:at + 6 * D].rearrange("p (s t n) -> p s t n", s=2, t=3)
        at = (at + 6 * D) // 2
        sel_f = w1_flat[:, at:at + T]
        xg = ga[:].rearrange("p a c t -> p (a c t)")[:, 0:2 * C * CAP].rearrange("p (s c t) -> p s c t", s=2, c=C)
        sel = ga[:].rearrange("p a c t -> p (a c t)")[:, 2 * C * CAP:2 * C * CAP + 3 * CAP].rearrange("p (t n) -> p t n", t=3)
        ye = gb[:].rearrange("p a c t -> p (a c t)")[:, 0:2 * D].rearrange("p (s n) -> p s n", s=2)
        sel_t = gb[:].rearrange("p a c t -> p (a c t)")[:, 2 * D:2 * D + T]
        mask_t, cum = var[0:NE, :], rtmp[0:NE, :]
        pb = ya
        ow = xa[:].rearrange("p c t -> p (c t)")[:, 0:UNIT]
        ub_flat = ub[:].rearrange("p c t -> p (c t)")
        xg_f = ub_flat[:, 0:C * CAP].rearrange("p (c t) -> p c t", c=C)
        hid_f = ub_flat[:, C * CAP:(C + EC) * CAP].rearrange("p (c t) -> p c t", c=EC)
        y_f = ub_flat[:, (C + EC) * CAP:(C + EC) * CAP + P]
        pair = sa[:].rearrange("p (k s c) t -> p k s c t", k=2, s=2)
        pair_g, pair_t = pair[:, 0], pair[:, 1]
        pair2 = sg[:].rearrange("p (k s c) t -> p k s c t", k=2, s=2)
        pair_u, pair_w = pair2[:, 0], pair2[:, 1]
        plew = side[:].rearrange("p a c n -> p (a c n)").rearrange("p (k n) -> p k n", k=PC)

        acc = ctx.enter_context(nc.psum_tensor("acc", [P, 4, 512], F32))
        aux = ctx.enter_context(nc.psum_tensor("aux", [P, 4, 512], F32))

        w_loaded = [sem(f"w_loaded{i}") for i in range(MOE_SLOTS)]
        hi_done, lo_done = sem("hi_done"), sem("lo_done")
        unit_mm = sem("unit_mm")
        evac_done = sem("evac_done")
        aux_full, aux_done = sem("aux_full"), sem("aux_done")
        ot_free, pair_free = sem("ot_free"), sem("pair_free")
        dv = sem("dv")
        vec_step, act_step = sem("vec_step"), sem("act_step")
        const_ready = sem("const_ready")
        small_loaded, x_loaded, p_loaded = sem("small_loaded"), sem("x_loaded"), sem("p_loaded")
        side_loaded = sem("side_loaded")
        sq_ready = sem("sq_ready")
        nf_ready, nh_ready, xn_ready = sem("nf_ready"), sem("nh_ready"), sem("xn_ready")
        ua_ready = sem("ua_ready")
        ga_ready, gb_ready, xm_ready = sem("ga_ready"), sem("gb_ready"), sem("xm_ready")
        st_ready, rows_out = sem("st_ready"), sem("rows_out")
        hid_ready = sem("hid_ready")
        mask_ready, pos_ready = sem("mask_ready"), sem("pos_ready")
        sel_ready, selt_ready = sem("sel_ready"), sem("selt_ready")
        gat_full, gat_done = sem("gat_full"), sem("gat_done")
        sc_full, sc_done = sem("sc_full"), sem("sc_done")
        csl_ready = sem("csl_ready")
        ys_ready = sem("ys_ready")
        sp_sel, sp_gat, sp_x, sp_csl = sem("sp_sel"), sem("sp_gat"), sem("sp_x"), sem("sp_csl")
        sp_w, sp_used = sem("sp_w"), sem("sp_used")
        sp_mm, sp_gu, sp_hid = sem("sp_mm"), sem("sp_gu"), sem("sp_hid")
        sp_ye, sp_sc, sp_h, sp_pass = sem("sp_ye"), sem("sp_sc"), sem("sp_h"), sem("sp_pass")
        y_out, old_out = sem("y_out"), sem("old_out")

        def v(name, layer=0, k=0):
            return ROWS[name][0] + layer + k

        N_CONST = 14 + NE

        AX_VEC = 2
        AX_H = AX_VEC + C
        AX_P = AX_H + LAYERS * PC
        AX_NORM, AX_GATES, AX_STATES, AX_PLE = [], [], [], []
        at = AX_P
        for l in range(LAYERS):
            AX_NORM.append(at + 1)
            AX_GATES.append(AX_NORM[-1] + 2 * C)
            AX_STATES.append(AX_GATES[-1] + 2)
            AX_NORM.append(AX_STATES[-1] + 1)
            at = AX_NORM[-1]
            if l == 1:
                AX_LOGITS = at + 1
                AX_NT = AX_LOGITS + 6
                AX_MASK = AX_NT + 1
                AX_POS = AX_MASK + 1
                AX_PB = at = AX_POS + NE
            AX_NORM.append(at + 1)
            AX_PLE.append(AX_NORM[-1] + C)
            at = AX_PLE[-1]
        AX_NORM.append(at + 1)
        AX_OUT = AX_NORM[-1]

        block = ctx.enter_context(nc.Block())

        @block.sync
        def _(sp):
            sp.dma_start(xrows[:, 0, :], a["x_prompt"][0, 0:P, :]).then_inc(x_loaded, 16)
            sp.dma_start(xrows[:, 1, :], a["x_prompt"][0, P:2 * P, :]).then_inc(x_loaded, 16)
            sp.dma_start(xrows[0:NSAMP, 2, :], a["x_sample"][:, 0, :]).then_inc(x_loaded, 16)

            def load(n, src, slot, k, it=None, step=0, slots=SLOTS):
                cols = src.shape[-1]
                if it is not None:
                    sp.wait_ge(hi_done, it * step + (n + 1 - slots))
                    sp.wait_ge(lo_done, it * step + (n + 1 - slots))
                elif n >= SLOTS:
                    sp.wait_ge(hi_done, n - LEAD)
                    sp.wait_ge(lo_done, n - LEAD)
                dst = raw_slot[slot][:, 0:k * cols].rearrange("p (c m) -> p c m", c=k)
                sp.dma_start(dst, src).then_inc(w_loaded[slot], 16)

            def matrix(w, n, k0=0):
                v_ = w.rearrange("(c p) m -> p c m", p=P)
                for u in range(SEC):
                    load(n + u, v_[:, k0:k0 + C, u * 256:(u + 1) * 256], u, C)

            def mixer(l):
                w = a["w_in"][l]
                by_section = w.rearrange("(c p) (s m) -> p c s m", p=P, s=IN_SECTIONS)
                n = N_MIX[l]
                matrix(w[:, 0:D], n)
                for first, count, col in IN_RUNS:
                    with sp.Fori(0, count) as s:
                        for u in range(SEC):
                            src = by_section[:, :, bass.ds(s + col, 1), u * 256:(u + 1) * 256]
                            load(n + SEC * first + u, src.rearrange("p c s m -> p c (s m)"), u, C, s, SEC)
                matrix(a["w_a_out"][l], N_MIX[l] + 28)
                matrix(a["w_b_out"][l], N_MIX[l] + 32)
                matrix(a["w_o"][l], N_MIX[l] + 36)

            mixer(0)
            gu = a["ffn_w_gu"][0].rearrange("(c p) (g i m) -> p c g i m", p=P, g=2, i=FFN_IT)
            with sp.Fori(0, FFN_IT) as it:
                for u in range(SEC):
                    g, half = u % 2, u // 2
                    src = gu[:, :, g, bass.ds(it, 1), half * 256:(half + 1) * 256].rearrange("p c i m -> p c (i m)")
                    load(N_GU + u, src, u, C, it, SEC)
            dn = a["ffn_w_dn"][0].rearrange("(g c p) m -> p g c m", p=P, g=3)
            with sp.Fori(0, 3) as it:
                for u in range(SEC):
                    src = dn[:, bass.ds(it, 1), :, u * 256:(u + 1) * 256].rearrange("p g c m -> p (g c) m")
                    load(N_DN + u, src, u, C, it, SEC)
            matrix(a["w_ple_gate"][0], N_PLE[0])
            mixer(1)
            n0 = N_MOE
            gu = a["moe_w_gu"][0].rearrange("e (c p) m -> p e c m", p=P)
            dn = a["moe_w_dn"][0].rearrange("e (c p) m -> p e c m", p=P)
            sp.wait_ge(hi_done, N_MOE)
            sp.wait_ge(lo_done, N_MOE)
            with sp.Fori(0, NE) as e:
                for u in range(MOE_GU):
                    if u == SLOTS:
                        sp.wait_ge(aux_full, AX_LOGITS)
                    col = (u % 2) * FE + (u // 2) * 256
                    load(n0 + u, gu[:, bass.ds(e, 1), :, col:col + 256].rearrange("p e c m -> p (e c) m"),
                         u % MOE_SLOTS, C, e, MOE_U, MOE_SLOTS)
                for u in range(MOE_DN):
                    half, k = u // 4, u % 4 * DN_K
                    src = dn[:, bass.ds(e, 1), k:k + DN_K, half * 512:(half + 1) * 512]
                    load(n0 + MOE_GU + u, src.rearrange("p e c m -> p (e c) m"), (MOE_GU + u) % MOE_SLOTS, DN_K, e,
                         MOE_U, MOE_SLOTS)
            matrix(a["w_ple_gate"][1], N_PLE[1])

            sp.wait_ge(aux_done, AX_OUT + 6)
            sp.dma_start(o["y_prompt"][0, 0:P, :], yrows[:, 0, :]).then_inc(y_out, 16)
            sp.dma_start(o["y_prompt"][0, P:2 * P, :], yrows[:, 1, :]).then_inc(y_out, 16)
            sp.dma_start(o["y_sample"][:, 0, :], yrows[0:NSAMP, 2, :]).then_inc(y_out, 16)
            sp.wait_ge(y_out, 48)

        @block.gpsimd
        def _(pool):
            nc.gpsimd.memset(side[:], 0.0).then_inc(const_ready, 1)
            nc.gpsimd.memset(ident[:], 0.0).then_inc(const_ready, 1)
            nc.gpsimd.memset(ones[:], 1.0).then_inc(const_ready, 1)
            nc.gpsimd.memset(eps[:], EPS).then_inc(const_ready, 1)
            nc.gpsimd.memset(tiny[:], 1e-30).then_inc(const_ready, 1)
            nc.gpsimd.memset(xa[:, :, 0:3], 0.0).then_inc(const_ready, 1)
            nc.gpsimd.memset(ub[:, :, 0:2], 0.0).then_inc(const_ready, 1)
            nc.gpsimd.memset(tri[:], 0.0).then_inc(const_ready, 1)
            nc.gpsimd.memset(lg[:], 0.0).then_inc(const_ready, 1)
            nc.gpsimd.memset(pos[:], -1.0).then_inc(const_ready, 1)
            nc.gpsimd.memset(prs[:], 0.0).then_inc(const_ready, 1)
            nc.gpsimd.iota(iota[:], pattern=[[1, CAP]], base=0, channel_multiplier=0,
                           allow_small_or_imprecise_dtypes=True).then_inc(const_ready, 1)
            nc.gpsimd.iota(slot_id[:], pattern=[[0, 1]], base=0, channel_multiplier=1,
                           allow_small_or_imprecise_dtypes=True).then_inc(const_ready, 1)
            pool.wait_ge(const_ready, 13)
            nc.gpsimd.affine_select(out=ident[:], in_=ident[:], compare_op=ALU.not_equal, fill=1.0, base=0,
                                    pattern=[[-1, P]], channel_multiplier=1).then_inc(const_ready, 1)
            for e in range(1, NE):
                nc.gpsimd.memset(tri[:, e, 0:e], 1.0).then_inc(const_ready, 1)
            pool.wait_ge(const_ready, 14)
            nc.gpsimd.tensor_copy(identh[:], ident[:]).then_inc(const_ready, 1)

            def side_gates(l):
                for g, w in enumerate((a["lru_wx"], a["lru_wa"])):
                    heads = w[l].rearrange("(c two) i j -> two i c j", two=2)
                    for k in range(2):
                        at = k * HB
                        pool.dma_start(side[at:at + HB, g, :, at:at + HB], heads[k]).then_inc(side_loaded, 16)

            side_gates(0)
            for l in range(LAYERS):
                pool.dma_start(o["conv_a_sample"][l, :, 0:2, :], a["state_conv_a"][l, :, 1:3, :]).then_inc(old_out, 16)
                pool.dma_start(o["conv_b_sample"][l, :, 0:1, :], a["state_conv_b"][l, :, 1:2, :]).then_inc(old_out, 16)
            for l in range(LAYERS):
                pool.wait_ge(aux_full, AX_GATES[l])
                pool.dma_start(plew, a["w_ple_proj"][l].rearrange("(k p) n -> p k n", p=P)).then_inc(side_loaded, 16)
                pool.wait_ge(aux_done, AX_STATES[l])
                for dst, r, n in ((o["conv_a_prompt"][l, 0], 0, 3), (o["conv_a_sample"][l, :, 2, :], 3, NSAMP),
                                  (o["conv_b_prompt"][l, 0], 11, 2), (o["conv_b_sample"][l, :, 1, :], 13, NSAMP),
                                  (o["lru_h_prompt"][l], 21, 1), (o["lru_h_sample"][l], 22, NSAMP)):
                    pool.dma_start(dst, rows[r:r + n, :]).then_inc(rows_out, 16)
                if l + 1 < LAYERS:
                    pool.wait_ge(aux_full, AX_PLE[l])
                    nc.gpsimd.memset(side[:], 0.0).then_inc(const_ready, 1)
                    pool.wait_ge(const_ready, N_CONST + 1)
                    side_gates(l + 1)
            pool.wait_ge(aux_done, AX_POS)
            spilled = pool.value_load(flag[0:1, 0:1], min_val=0, max_val=1)
            gu = a["moe_w_gu"][0].rearrange("e (c p) (g j m) -> p e g j c m", p=P, g=2, j=EC)
            dn = a["moe_w_dn"][0].rearrange("e (c p) (j m) -> p e j c m", p=P, j=C)
            with pool.If(spilled > 0):
                with pool.Fori(0, SPILLS) as p:
                    with pool.Fori(0, NE) as e:
                        with pool.Fori(0, EC) as j:
                            pool.wait_ge(sp_used, (p * NE + e) * (EC + C) + (j + 1))
                            for g in range(2):
                                src = gu[:, bass.ds(e, 1), g, bass.ds(j, 1), :, :]
                                pool.dma_start(ow[:, g * 1024:(g + 1) * 1024].rearrange("p (c m) -> p c m", c=C),
                                               src.rearrange("p e j c m -> p (e j c) m")).then_inc(sp_w, 16)
                        with pool.Fori(0, C) as j:
                            pool.wait_ge(sp_used, (p * NE + e) * (EC + C) + (j + (EC + 1)))
                            src = dn[:, bass.ds(e, 1), bass.ds(j, 1), :, :]
                            for g in range(2):
                                c = EC // 2
                                pool.dma_start(ow[:, g * c * P:(g + 1) * c * P].rearrange("p (c m) -> p c m", c=c),
                                               src[:, :, :, g * c:(g + 1) * c].rearrange("p e j c m -> p (e j c) m")
                                               ).then_inc(sp_w, 16)
            with pool.Else():
                pool.nop()
            pool.wait_ge(rows_out, 16 * 6 * LAYERS)
            pool.wait_ge(old_out, 32 * LAYERS)

        @block.tensor
        def _(pe):
            ax = [0]

            def aux_bank():
                i = ax[0]
                ax[0] += 1
                if i >= 4:
                    pe.wait_ge(aux_done, i - 3)
                return aux[:, i % 4, :]

            def unit(n, slot, half, x, k_chunks, cols, x0=0, at=None, it=None, step=0):
                extra = 0 if it is None else it * step
                if it is not None:
                    pe.wait_ge(evac_done, extra + (n - 1))
                    pe.wait_ge(hi_done, extra + (n + 1))
                    pe.wait_ge(lo_done, extra + (n + 1))
                else:
                    if n >= 2:
                        pe.wait_ge(evac_done, n - 1 - (UNCOUNTED if n >= N_PLE[1] else 0))
                    pe.wait_ge(hi_done, n + 1)
                    pe.wait_ge(lo_done, n + 1)
                th = wh[:, slot, 0:k_chunks * cols].rearrange("p (c m) -> p c m", c=k_chunks)
                tl = wl[:, slot, 0:k_chunks * cols].rearrange("p (c m) -> p c m", c=k_chunks)
                for m in range(cols // P):
                    bank = acc[:, 2 * half + m, 0:T]
                    for k in range(k_chunks):
                        if m == 0 and at and k in at:
                            pe.wait_ge(*at[k])
                        hi, lo = th[:, k, m * P:(m + 1) * P], tl[:, k, m * P:(m + 1) * P]
                        nc.tensor.matmul(bank, hi, x[:, 0, x0 + k, :], start=(k == 0), stop=False)
                        nc.tensor.matmul(bank, hi, x[:, 1, x0 + k, :], start=False, stop=False)
                        last = nc.tensor.matmul(bank, lo, x[:, 0, x0 + k, :], start=False, stop=(k == k_chunks - 1))
                last.then_inc(unit_mm, 1)

            def matrix(n, x, ready=None, base=0):
                at = {2 * i: (ready, base + i + 1) for i in range(C // 2)} if ready is not None else None
                for u in range(SEC):
                    unit(n + u, u, u % 2, x, C, 256, at=at if u == 0 else None)

            def sections(n, count, x):
                with pe.Fori(0, count) as s:
                    for u in range(SEC):
                        unit(n + u, u, u % 2, x, C, 256, it=s, step=SEC)

            norms = [0]

            def norm_stats():
                k = norms[0]
                norms[0] += 1
                bank = aux_bank()
                for c in range(C):
                    if c % 2 == 0:
                        pe.wait_ge(sq_ready, 4 * k + c // 2 + 1)
                    last = nc.tensor.matmul(bank[:, 0:T], ones[:], sq[:, c, :], start=(c == 0), stop=(c == C - 1))
                last.then_inc(aux_full, 1)

            pe.wait_ge(const_ready, N_CONST)
            pe.wait_ge(small_loaded, 16 * (len(ROWS) + 1))
            for g in range(2):
                bank = aux_bank()
                for c in range(4):
                    last = nc.tensor.transpose(bank[:, c * P:c * P + N_ROWS], vrows[0:N_ROWS, (4 * g + c) * P:(4 * g + c + 1) * P],
                                               ident[0:N_ROWS, 0:N_ROWS])
                last.then_inc(aux_full, 1)

            def columns(bank, src, c):
                nc.tensor.transpose(bank[:, 0:P], src[:, 0, c * P:(c + 1) * P], ident[:])
                nc.tensor.transpose(bank[:, P:2 * P], src[:, 1, c * P:(c + 1) * P], ident[:])
                return nc.tensor.transpose(bank[:, SEQ:T], src[0:NSAMP, 2, c * P:(c + 1) * P], ident[0:NSAMP, 0:NSAMP])

            pe.wait_ge(x_loaded, 48)
            for c in range(C):
                columns(aux_bank(), xrows, c).then_inc(aux_full, 1)
            pe.wait_ge(p_loaded, 16 * 3 * LAYERS)
            for l in range(LAYERS):
                for c in range(PC):
                    columns(aux_bank(), prows[:, l], c).then_inc(aux_full, 1)

            def mixer(l):
                n0 = N_MIX[l]
                norm_stats()
                matrix(n0, xn, xn_ready, 4 * 3 * l)
                sections(n0 + SEC, 2, xn)
                pe.wait_ge(ua_ready, l + 1)
                pe.wait_ge(side_loaded, 16 * (5 * l + 4))
                for g in range(2):
                    for c in range(C):
                        last = nc.tensor.matmul(aux_bank()[:, 0:T], side[:, g, c, :], ua[:, c, :], start=True, stop=True)
                        last.then_inc(aux_full, 1)
                sections(n0 + 3 * SEC, 4, xn)
                pe.wait_ge(st_ready, l + 1)
                for g in range(2):
                    bank = aux_bank()
                    for c in range(4):
                        last = nc.tensor.transpose(bank[0:30, c * P:(c + 1) * P], st[:, 4 * g + c, :], ident[:])
                    last.then_inc(aux_full, 1)
                matrix(n0 + 28, ga, ga_ready, 4 * l)
                matrix(n0 + 32, gb, gb_ready, 4 * l)
                matrix(n0 + 36, xn, xm_ready, 4 * l)

            def ple(l, n):
                norm_stats()
                pe.wait_ge(side_loaded, 16 * 5 * (l + 1))
                for m in range(C):
                    bank = aux_bank()
                    for k in range(PC):
                        last = nc.tensor.matmul(bank[:, 0:T], plew[:, k, m * P:(m + 1) * P], pt[:, l, k, :],
                                                start=(k == 0), stop=(k == PC - 1))
                    last.then_inc(aux_full, 1)
                matrix(n, xn, xn_ready, 4 * (3 * l + 2))

            mixer(0)
            norm_stats()
            matrix(N_GU, xn, xn_ready, 4)
            sections(N_GU + SEC, FFN_IT - 1, xn)
            for k in range(3):
                for u in range(SEC):
                    at = {2 * i: (hid_ready, 4 * k + i + 1) for i in range(4)} if u == 0 else None
                    unit(N_DN + SEC * k + u, u, u % 2, hid, C, 256, x0=C * k, at=at)
            ple(0, N_PLE[0])

            mixer(1)
            norm_stats()
            pe.wait_ge(xn_ready, 4 * 5)
            bank = aux_bank()
            for t, (lo, n) in enumerate(TOK):
                for c in range(C):
                    last = nc.tensor.matmul(bank[0:n, t * NE:(t + 1) * NE], nf[:, c, lo:lo + n], rt[:, c, :],
                                            start=(c == 0), stop=(c == C - 1))
            last.then_inc(aux_full, 1)
            for s in range(2):
                for t, (lo, n) in enumerate(TOK):
                    bank = aux_bank().bitcast(F16)
                    for c in range(C):
                        last = nc.tensor.transpose(bank[0:n, c * P:(c + 1) * P], xn[:, s, c, lo:lo + n], identh[:])
                    last.then_inc(aux_full, 1)
            pe.wait_ge(mask_ready, 1)
            bank = aux_bank()
            for t, (lo, n) in enumerate(TOK):
                last = nc.tensor.transpose(bank[0:NE, lo:lo + n], rank[0:n, t, :], ident[0:n, 0:n])
            last.then_inc(aux_full, 1)
            pe.wait_ge(pos_ready, 1)
            bank = aux_bank()
            for t, (lo, n) in enumerate(TOK):
                nc.tensor.transpose(bank[0:n, t * NE:(t + 1) * NE], cum[:, lo:lo + n], ident[0:NE, 0:NE])
            nc.tensor.matmul(bank[0:1, 3 * NE:3 * NE + 1], over[:], ones[0:NE, 0:1], start=True,
                             stop=True).then_inc(aux_full, 1)
            for e in range(NE):
                bank = aux_bank()
                nc.tensor.matmul(bank[0:CAP, 0:T], ident[0:NE, e:e + 1].to_broadcast([NE, CAP]), cum, start=True,
                                 stop=True).then_inc(aux_full, 1)

            pe.wait_ge(aux_done, AX_PB)
            spilled = pe.value_load(flag[0:1, 0:1], min_val=0, max_val=1)
            with pe.If(spilled > 0):
                with pe.Fori(0, SPILLS) as p:
                    with pe.Fori(0, NE) as e:
                        q = p * NE + e
                        pe.wait_ge(sp_sel, q + 1)
                        pe.wait_ge(sp_h, q * C + 1)
                        for c in range(C):
                            bank = aux[:, c // 4, (c % 4) * CAP:(c % 4 + 1) * CAP]
                            for i in range(6):
                                t, n = i // 2, TOK[i // 2][1]
                                nc.tensor.matmul(bank, nt[0:n, i % 2, t, c * P:(c + 1) * P], sel[0:n, t, :],
                                                 start=(i == 0), stop=(i == 5))
                        for t, (_, n) in enumerate(TOK):
                            last = nc.tensor.matmul(aux[0:CAP, 2, 0:2], sel[0:n, t, :], prs_e[0:n, t, :],
                                                    start=(t == 0), stop=(t == 2))
                        last.then_inc(sp_gat, 1)
                        with pe.Fori(0, EC) as j:
                            pe.wait_ge(sp_x, q + 1)
                            pe.wait_ge(sp_w, (q * (EC + C) + j) * 32 + 32)
                            pe.wait_ge(sp_gu, q * EC + (j + 1))
                            for g in range(2):
                                for k in range(C):
                                    w = ow[:, g * 1024 + k * P:g * 1024 + (k + 1) * P]
                                    last = nc.tensor.matmul(acc[:, g, 0:CAP], w, xg_f[:, k, :], start=(k == 0),
                                                            stop=(k == C - 1))
                            last.then_inc(sp_used, 1)
                        with pe.Fori(0, C) as j:
                            pe.wait_ge(sp_hid, (q + 1) * EC + 1)
                            pe.wait_ge(sp_w, (q * (EC + C) + j) * 32 + (EC + 1) * 32)
                            for k in range(EC):
                                last = nc.tensor.matmul(acc[0:CAP, 2, 0:P], hid_f[:, k, :], ow[:, k * P:(k + 1) * P],
                                                        start=(k == 0), stop=(k == EC - 1))
                            last.then_inc(sp_used, 1)
                            pe.wait_ge(sp_ye, q * C + (j + 1))
                            pe.wait_ge(sp_h, q * C + (j + 1))
                            nc.tensor.matmul(acc[:, 3, 0:T], y_f[0:CAP, :], sel_f[0:CAP, :], start=True,
                                             stop=True).then_inc(sp_sc, 1)
                pe.wait_ge(sp_h, SPILLS * NE * C + 1)
            with pe.Else():
                pe.nop()

            def gather(adds):
                for g in range(4):
                    pe.wait_ge(sc_done, adds(g + 5))
                    for c in (2 * g, 2 * g + 1):
                        for s in range(2):
                            at = (c % 2 * 2 + s) * CAP
                            for t, (_, n) in enumerate(TOK):
                                last = nc.tensor.matmul(aux[:, g, at:at + CAP], nt[0:n, s, t, c * P:(c + 1) * P],
                                                        sel[0:n, t, :], start=(t == 0), stop=(t == 2))
                    if g == 3:
                        for t, (_, n) in enumerate(TOK):
                            last = nc.tensor.matmul(aux[0:CAP, g, 4 * CAP:4 * CAP + 2], sel[0:n, t, :], prs_e[0:n, t, :],
                                                    start=(t == 0), stop=(t == 2))
                    last.then_inc(gat_full, 1)

            def scatter(chunks, free):
                for c in chunks:
                    free(c)
                    nc.tensor.matmul(aux[:, c % 4, 0:T], ye[0:CAP, 0, c * P:(c + 1) * P], sel_t[0:CAP, :],
                                     start=True, stop=False)
                    nc.tensor.matmul(aux[:, c % 4, 0:T], ye[0:CAP, 1, c * P:(c + 1) * P], sel_t[0:CAP, :],
                                     start=False, stop=True).then_inc(sc_full, 1)

            pe.wait_ge(sel_ready, 1)
            gather(lambda i: i)
            with pe.Fori(0, NE) as e:
                pe.wait_ge(gat_done, e * 4 + 4)
                for u in range(MOE_GU):
                    n = N_MOE + u
                    pe.wait_ge(evac_done, e * MOE_EVAC + (n - 1))
                    pe.wait_ge(hi_done, e * MOE_U + (n + 1))
                    pe.wait_ge(lo_done, e * MOE_U + (n + 1))
                    th = wh[:, u % SLOTS, :].rearrange("p (c m) -> p c m", c=C)
                    tl = wl[:, u % SLOTS, :].rearrange("p (c m) -> p c m", c=C)
                    for m in range(2):
                        bank = acc[:, u % 2, m * CAP:(m + 1) * CAP]
                        for k in range(C):
                            hi, lo = th[:, k, m * P:(m + 1) * P], tl[:, k, m * P:(m + 1) * P]
                            nc.tensor.matmul(bank, hi, xg[:, 0, k, :], start=(k == 0), stop=False)
                            nc.tensor.matmul(bank, hi, xg[:, 1, k, :], start=False, stop=False)
                            last = nc.tensor.matmul(bank, lo, xg[:, 0, k, :], start=False, stop=(k == C - 1))
                    last.then_inc(unit_mm, 1)
                    if u == 1:
                        pe.wait_ge(ys_ready, e * 2 + 2)
                        pe.wait_ge(selt_ready, e + 1)
                        scatter(range(4), lambda i: None)
                    if u in (4, 6):
                        scatter(range(u, u + 2), lambda i: pe.wait_ge(sc_done, e * 8 + (8 + i - 3)))
                pe.wait_ge(sel_ready, e + 2)
                gather(lambda i: e * 8 + (i + 8))
                for u in range(MOE_DN):
                    n = N_MOE + MOE_GU + u
                    half, k0 = u // 4, u % 4 * DN_K
                    pe.wait_ge(hi_done, e * MOE_U + (n + 1))
                    pe.wait_ge(lo_done, e * MOE_U + (n + 1))
                    if k0 == 0:
                        pe.wait_ge(ys_ready, e * 2 + (half + 1))
                    th = wh[:, u % SLOTS, 0:DN_K * 512].rearrange("p (c m) -> p c m", c=DN_K)
                    tl = wl[:, u % SLOTS, 0:DN_K * 512].rearrange("p (c m) -> p c m", c=DN_K)
                    for k in range(DN_K):
                        if half == 0 and (k0 + k) % 2 == 0:
                            pe.wait_ge(hid_ready, e * 6 + (FFN_IT * 2 + (k0 + k) // 2 + 1))
                        bank = acc[0:CAP, 2 + half, :]
                        first, end = k0 + k == 0, k0 + k == EC - 1
                        nc.tensor.matmul(bank, hid_e[:, 0, k0 + k, :], th[:, k, :], start=first, stop=False)
                        nc.tensor.matmul(bank, hid_e[:, 0, k0 + k, :], tl[:, k, :], start=False, stop=False)
                        last = nc.tensor.matmul(bank, hid_e[:, 1, k0 + k, :], th[:, k, :], start=False, stop=end)
                    last.then_inc(unit_mm, 1)
            pe.wait_ge(ys_ready, 2 * NE + 2)
            pe.wait_ge(selt_ready, NE + 1)
            pe.wait_ge(gat_done, 4 * NE + 4)
            scatter(range(8), lambda i: pe.wait_ge(sc_done, 8 + 8 * NE + i - 3) if i >= 4 else None)
            pe.wait_ge(sc_done, 8 * NE + 16)
            ple(1, N_PLE[1])

            norm_stats()
            pe.wait_ge(nf_ready, 4 * 7)
            for t, (lo, n) in enumerate(((0, P), (P, P), (SEQ, NSAMP))):
                for g in range(2):
                    bank = aux_bank()
                    for c in range(4):
                        last = nc.tensor.transpose(bank[0:n, c * P:(c + 1) * P], nf[:, 4 * g + c, lo:lo + n], ident[:])
                    last.then_inc(aux_full, 1)

        @block.scalar
        def _(act):
            small = [(name, a[name]) for name in ROWS]
            for name, ap in small:
                r, n = ROWS[name]
                if len(ap.shape) == 1:
                    src = ap.rearrange("(a n) -> a n", a=1)
                elif len(ap.shape) == 2:
                    src = ap
                elif len(ap.shape) == 3:
                    src = ap.rearrange("a b n -> (a b) n")
                else:
                    src = ap.rearrange("a b c n -> (a b c) n")
                act.dma_start(vrows[r:r + n, :], src).then_inc(small_loaded, 16)
            act.dma_start(rt[:], a["router"][0].rearrange("(c p) e -> p c e", p=P)).then_inc(small_loaded, 16)
            for l in range(LAYERS):
                act.dma_start(prows[:, l, 0, :], a["p_prompt"][l, 0, 0:P, :]).then_inc(p_loaded, 16)
                act.dma_start(prows[:, l, 1, :], a["p_prompt"][l, 0, P:2 * P, :]).then_inc(p_loaded, 16)
                act.dma_start(prows[0:NSAMP, l, 2, :], a["p_sample"][l, :, 0, :]).then_inc(p_loaded, 16)

            ax, ots, prs = [0], [0], [0]

            def aux_bank():
                i = ax[0]
                ax[0] += 1
                act.wait_ge(aux_full, i + 1)
                return aux[:, i % 4, :]

            def hi(n, size=UNIT, it=None, step=0):
                s = n % SLOTS
                from_slot, turn = raw_turn(n)
                extra = 0 if it is None else it * step
                per_turn = 0 if it is None else step // (SLOTS if step == SEC else MOE_SLOTS)
                act.wait_ge(w_loaded[from_slot], 16 * turn if it is None else it * (16 * per_turn) + 16 * turn)
                if n >= SLOTS:
                    act.wait_ge(unit_mm, (n - LEAD) if it is None else extra + (n - LEAD))
                nc.scalar.activation(wh[:, s, 0:size], raw_slot[from_slot][:, 0:size], ACT.Copy, scale=WS).then_inc(hi_done, 1)

            def psum_ready(n, it=None, step=0):
                act.wait_ge(unit_mm, n + 1 if it is None else it * step + (n + 1))
                return acc[:, 2 * (n % 2):2 * (n % 2) + 2, 0:T]

            def tell():
                return act_step, 1

            vec_seen = [0]

            def from_vector():
                vec_seen[0] += 1
                act.wait_ge(vec_step, vec_seen[0])

            def stats():
                nc.scalar.activation(root[:], eps[:], ACT.Sqrt)
                bank = aux_bank()
                nc.scalar.activation(std[:], bank[:, 0:T], ACT.Sqrt, bias=eps[:], scale=1.0 / D)
                nc.scalar.activation(var[:], bank[:, 0:T], ACT.Identity, bias=eps[:], scale=1.0 / D).then_inc(aux_done, 1)

            norm = [0]

            def norm_hi():
                for i in range(C // 2):
                    act.wait_ge(nf_ready, 4 * norm[0] + i + 1)
                    nc.scalar.activation(xn[:, 0, 2 * i:2 * i + 2, :], nf[:, 2 * i:2 * i + 2, :], ACT.Copy,
                                         scale=XS).then_inc(nh_ready, 1)
                norm[0] += 1

            def evac(n, dst, func=ACT.Copy, scale=UNSCALE):
                nc.scalar.activation(dst, psum_ready(n), func, scale=scale).then_inc(evac_done, 1)

            def evac_ot(n):
                if ots[0] >= 2:
                    act.wait_ge(ot_free, ots[0] - 1)
                evac(n, ot[:, ots[0] % 2])
                ots[0] += 1

            act.wait_ge(const_ready, N_CONST)
            for n in range(LEAD):
                hi(n)
            for g in range(2):
                nc.scalar.activation(vec[:, 4 * g:4 * g + 4, 0:N_ROWS],
                                     aux_bank().rearrange("p (c r) -> p c r", c=4)[:, :, 0:N_ROWS],
                                     ACT.Copy).then_inc(aux_done, 1)
            for c in range(C):
                nc.scalar.activation(h[:, c, :], aux_bank()[:, 0:T], ACT.Copy).then_inc(aux_done, 1)
            for l in range(LAYERS):
                for c in range(PC):
                    nc.scalar.activation(pt[:, l, c, :], aux_bank()[:, 0:T], ACT.Copy).then_inc(aux_done, 1)
            from_vector()
            nc.scalar.activation(lam_b[:], lam_a[:], ACT.Exp, scale=-1.0).then_inc(*tell())

            def mixer(l):
                n0 = N_MIX[l]
                stats()
                norm_hi()
                for u in range(SEC):
                    hi(n0 + u + LEAD)
                    evac(n0 + u, xa[:, 2 * u:2 * u + 2, 3:3 + T])
                n = n0 + SEC
                for u in range(SEC):
                    hi(n + u + LEAD)
                    evac(n + u, ya[:, 2 * u:2 * u + 2, :])
                n += SEC
                for u in range(SEC):
                    hi(n + u + LEAD)
                    evac(n + u, xb[:, 2 * u:2 * u + 2, :])
                    if u == 1:
                        from_vector()
                        nc.scalar.activation(gx, gx, ACT.Tanh).then_inc(*tell())
                from_vector()
                for g, dst in enumerate((gx, gy)):
                    for c in range(C):
                        last = nc.scalar.activation(dst[:, c, :], aux_bank()[:, 0:T], ACT.Tanh, scale=0.5,
                                                    bias=hb[:, c, 2 * g + l:2 * g + l + 1])
                        last.then_inc(aux_done, 1)
                n += SEC
                for u in range(SEC):
                    hi(n + u + LEAD)
                    evac(n + u, ub[:, 2 * u:2 * u + 2, 2:2 + T])
                from_vector()
                nc.scalar.activation(gb_f, gy, ACT.Exp, scale=-1.0)
                nc.scalar.activation(ga_f, gy, ACT.Tanh, bias=tiny[:]).then_inc(*tell())
                n += SEC
                for u in range(SEC):
                    hi(n + u + LEAD)
                    evac_ot(n + u)
                    if u == 2:
                        from_vector()
                        nc.scalar.activation(gy, gy, ACT.Sqrt).then_inc(*tell())
                n += SEC
                for dst in (sa, sg):
                    for u in range(SEC):
                        hi(n + u + LEAD)
                        evac(n + u, dst[:, 2 * u:2 * u + 2, :], ACT.Tanh, 0.5 * UNSCALE)
                    n += SEC
                if l:
                    act.wait_ge(rows_out, 16 * 6 * l)
                for g in range(2):
                    nc.scalar.activation(rows[0:30, g * 512:(g + 1) * 512], aux_bank()[0:30, :],
                                         ACT.Copy).then_inc(aux_done, 1)
                for _ in range(3):
                    for u in range(SEC):
                        hi(n + u + LEAD)
                        evac_ot(n + u)
                    n += SEC

            def ple(l, n):
                stats()
                for m in range(4):
                    nc.scalar.activation(ya[:, m, :], aux_bank()[:, 0:T], ACT.Copy).then_inc(aux_done, 1)
                norm_hi()
                for m in range(4, C):
                    last = nc.scalar.activation(ya[:, m, :], aux_bank()[:, 0:T], ACT.Copy)
                    last.then_inc(aux_done, 1)
                for u in range(SEC):
                    if n + u + LEAD < N_END:
                        hi(n + u + LEAD)
                    if ots[0] >= 2:
                        act.wait_ge(ot_free, ots[0] - 1)
                    evac(n + u, ot[:, ots[0] % 2], ACT.Tanh, 0.5 * UNSCALE)
                    ots[0] += 1

            def gate_up(n, u, p, it, step, pairs):
                src = psum_ready(n, it, step)
                s = p % 2
                if u % 2 == 0:
                    act.wait_ge(pair_free, it * pairs + (prs[0] + p + 1))
                    nc.scalar.activation(pair_g[:, s], src, ACT.Copy, scale=UNSCALE)
                    nc.scalar.activation(pair_t[:, s], src, ACT.Tanh, scale=0.5 * UNSCALE).then_inc(evac_done, 1)
                else:
                    nc.scalar.activation(pair_u[:, s], src, ACT.Copy, scale=UNSCALE).then_inc(evac_done, 1)

            mixer(0)
            stats()
            norm_hi()
            with act.Fori(0, FFN_IT) as it:
                for u in range(SEC):
                    hi(N_GU + u + LEAD, it=it, step=SEC)
                    gate_up(N_GU + u, u, u // 2, it, SEC, 2)
            prs[0] += 2 * FFN_IT
            for k in range(3):
                for u in range(SEC):
                    n = N_DN + SEC * k + u
                    hi(n + LEAD)
                    evac_ot(n)
            ple(0, N_PLE[0])
            mixer(1)
            stats()
            norm_hi()
            bank = aux_bank()
            nc.scalar.activation(lg[:, 0:2, :], bank[:, 0:2 * NE].rearrange("p (t e) -> p t e", e=NE), ACT.Copy)
            nc.scalar.activation(lg[0:NSAMP, 2, :], bank[0:NSAMP, 2 * NE:3 * NE], ACT.Copy).then_inc(aux_done, 1)

            def rows_of_tokens(fills):
                for i in fills:
                    n = TOK[i % 3][1]
                    nc.scalar.activation(nt[0:n, i // 3, i % 3, :], aux_bank().bitcast(F16)[0:n, :],
                                         ACT.Copy).then_inc(aux_done, 1)

            rows_of_tokens(range(4))
            from_vector()
            nc.scalar.activation(pr[:], pr[:], ACT.Exp).then_inc(*tell())
            rows_of_tokens(range(4, 6))
            nc.scalar.activation(mask_t, aux_bank()[0:NE, 0:T], ACT.Copy).then_inc(aux_done, 1)
            bank = aux_bank()
            for t, (_, n) in enumerate(TOK):
                nc.scalar.activation(pos[0:n, t, 0:NE], bank[0:n, t * NE:(t + 1) * NE], ACT.Copy)
            nc.scalar.activation(flag[:], bank[0:1, 3 * NE:3 * NE + 1], ACT.Sign).then_inc(aux_done, 1)
            for e in range(NE):
                nc.scalar.activation(pb[0:CAP, e, :], aux_bank()[0:CAP, 0:T], ACT.Copy).then_inc(aux_done, 1)

            act.wait_ge(aux_done, AX_POS)
            spilled = act.value_load(flag[0:1, 0:1], min_val=0, max_val=1)
            with act.If(spilled > 0):
                with act.Fori(0, SPILLS) as p:
                    with act.Fori(0, NE) as e:
                        q = p * NE + e
                        act.wait_ge(sp_gat, q + 1)
                        for g in range(2):
                            nc.scalar.activation(xg_f[:, 4 * g:4 * g + 4, :],
                                                 aux[:, g, 0:4 * CAP].rearrange("p (c t) -> p c t", c=4),
                                                 ACT.Copy, scale=1.0 / XS)
                        nc.scalar.activation(csr[0:CAP, :], aux[0:CAP, 2, 0:2], ACT.Copy).then_inc(sp_x, 1)
                        with act.Fori(0, EC) as j:
                            act.wait_ge(sp_used, q * (EC + C) + (j + 2))
                            act.wait_ge(sp_hid, q * EC + (j + 1))
                            nc.scalar.activation(pair_g[:, 0, 0, 0:CAP], acc[:, 0, 0:CAP], ACT.Copy)
                            nc.scalar.activation(pair_t[:, 0, 0, 0:CAP], acc[:, 0, 0:CAP], ACT.Tanh, scale=0.5)
                            nc.scalar.activation(pair_u[:, 0, 0, 0:CAP], acc[:, 1, 0:CAP],
                                                 ACT.Copy).then_inc(sp_gu, 1)
                        with act.Fori(0, C) as j:
                            act.wait_ge(sp_csl, q + 1)
                            act.wait_ge(sp_used, q * (EC + C) + (j + (EC + 2)))
                            nc.scalar.activation(y_f[0:CAP, :], acc[0:CAP, 2, 0:P], ACT.Identity,
                                                 scale=csl[0:CAP, :]).then_inc(sp_ye, 1)
                            act.wait_ge(sp_sc, q * C + (j + 1))
            with act.Else():
                act.nop()

            def gathered(fills, seen):
                for g in fills:
                    act.wait_ge(gat_full, seen(g + 1))
                    last = nc.scalar.activation(xg[:, :, 2 * g:2 * g + 2, :].rearrange("p s c t -> p c s t"),
                                                aux[:, g, 0:4 * CAP].rearrange("p (c s t) -> p c s t", c=2, s=2),
                                                ACT.Copy)
                    if g == 3:
                        last = nc.scalar.activation(csr[0:CAP, :], aux[0:CAP, g, 4 * CAP:4 * CAP + 2], ACT.Copy)
                    last.then_inc(gat_done, 1)

            gathered(range(4), lambda i: i)
            with act.Fori(0, NE) as e:
                for u in range(MOE_GU):
                    n = N_MOE + u
                    hi(n + LEAD, moe_unit_size(u + LEAD), e, MOE_U)
                    act.wait_ge(unit_mm, e * MOE_U + (n + 1))
                    src = acc[:, u % 2, 0:2 * CAP].rearrange("p (c t) -> p c t", c=2)
                    k = u // 2 % 2
                    if u % 2 == 0:
                        act.wait_ge(pair_free, e * 6 + (2 * FFN_IT + u // 2 + 1))
                        nc.scalar.activation(pair_g[:, k, :, 0:CAP], src, ACT.Copy, scale=UNSCALE)
                        nc.scalar.activation(pair_t[:, k, :, 0:CAP], src, ACT.Tanh,
                                             scale=0.5 * UNSCALE).then_inc(evac_done, 1)
                    else:
                        nc.scalar.activation(pair_u[:, k, :, 0:CAP], src, ACT.Copy, scale=UNSCALE).then_inc(evac_done, 1)
                for u in range(MOE_DN):
                    n = N_MOE + MOE_GU + u
                    hi(n + LEAD, moe_unit_size(MOE_GU + u + LEAD), e, MOE_U)
                    if u < 2:
                        gathered((2 * u, 2 * u + 1), lambda i: e * 4 + (i + 4))
                    if u in (4, 7):
                        half = u // 5
                        act.wait_ge(unit_mm, e * MOE_U + (N_MOE + MOE_GU + 4 * half + 4))
                        act.wait_ge(csl_ready, e + 1)
                        act.wait_ge(sc_full, e * 8 + 8)
                        nc.scalar.activation(ye[0:CAP, 0, half * 512:(half + 1) * 512], acc[0:CAP, 2 + half, :],
                                             ACT.Identity, scale=csl[0:CAP, :]).then_inc(evac_done, 1)
            ple(1, N_PLE[1])
            stats()
            for t, n in enumerate((P, P, NSAMP)):
                for g in range(2):
                    nc.scalar.activation(yrows[0:n, t, g * 512:(g + 1) * 512], aux_bank()[0:n, :],
                                         ACT.Copy).then_inc(aux_done, 1)

        @block.vector
        def _(vec_e):
            V = nc.vector
            count = {}
            loop = [None, {}]
            prev = [None]

            def op(ins, s=dv, by=1):
                count[s] = count.get(s, 0) + by
                ins.then_inc(s, by)
                prev[0] = s

            def settle():
                s = prev[0]
                vec_e.wait_ge(s, count[s] if loop[0] is None else loop[0] * loop[1][s] + count[s])

            def lo(n, size=UNIT, it=None, step=0):
                s = n % SLOTS
                vec_e.wait_ge(hi_done, n + 1 if it is None else it * step + (n + 1))
                op(V.scalar_tensor_tensor(out=wl[:, s, 0:size], in0=raw_slot[raw_turn(n)[0]][:, 0:size], scalar=WS,
                                          in1=wh[:, s, 0:size], op0=ALU.mult, op1=ALU.subtract), lo_done)

            def evacuated(n, it=None, step=0):
                n += 1 - (UNCOUNTED if n >= N_PLE[1] else 0)
                vec_e.wait_ge(evac_done, n if it is None else it * step + n)

            act_seen = [0]

            def from_scalar():
                act_seen[0] += 1
                vec_e.wait_ge(act_step, act_seen[0])

            def col(row, c):
                return vec[:, c, row:row + 1]

            def cols(row, n):
                return vec[:, :, row:row + 1].to_broadcast([P, C, n])

            def square(i):
                op(V.tensor_tensor(sq[:, 2 * i:2 * i + 2, :], h[:, 2 * i:2 * i + 2, :], h[:, 2 * i:2 * i + 2, :],
                                   ALU.mult), sq_ready)

            norms = [0]

            def norm(gain, split=True):
                k = norms[0]
                norms[0] += 1
                vec_e.wait_ge(aux_done, AX_NORM[k])
                op(V.reciprocal(rstd[:], std[:]))
                settle()
                op(V.tensor_tensor(rtmp[:], rstd[:], rstd[:], ALU.mult))
                settle()
                op(V.scalar_tensor_tensor(out=rtmp[:], in0=rtmp[:], scalar=-0.5, in1=var[:], op0=ALU.mult, op1=ALU.mult))
                settle()
                op(V.scalar_tensor_tensor(out=rstd[:], in0=rtmp[:], scalar=1.5, in1=rstd[:], op0=ALU.add, op1=ALU.mult))
                settle()

                def low(i):
                    vec_e.wait_ge(nh_ready, 4 * k + i + 1)
                    s = slice(2 * i, 2 * i + 2)
                    op(V.scalar_tensor_tensor(out=xn[:, 1, s, :], in0=nf[:, s, :], scalar=XS, in1=xn[:, 0, s, :],
                                              op0=ALU.mult, op1=ALU.subtract), xn_ready)

                for i in range(C // 2):
                    for c in (2 * i, 2 * i + 1):
                        op(V.scalar_tensor_tensor(out=nf[:, c, :], in0=h[:, c, :], scalar=col(gain, c), in1=rstd[:],
                                                  op0=ALU.mult, op1=ALU.mult), dv if c % 2 == 0 else nf_ready)
                    if split and i:
                        low(i - 1)
                if split:
                    low(C // 2 - 1)

            def conv(out, src, taps, row, bias, u):
                two = (2 * u, 2 * u + 1)
                for j in range(taps):
                    for c in two:
                        if j == 0 and bias is None:
                            i = V.tensor_scalar(out[:, c, 0:SEQ], src[:, c, 0:SEQ], col(row, c), None, ALU.mult)
                        elif j == 0:
                            i = V.tensor_scalar(out[:, c, 0:SEQ], src[:, c, 0:SEQ], col(row, c), col(bias, c),
                                                ALU.mult, ALU.add)
                        else:
                            i = V.scalar_tensor_tensor(out=out[:, c, 0:SEQ], in0=src[:, c, j:j + SEQ],
                                                       scalar=col(row + j, c), in1=out[:, c, 0:SEQ],
                                                       op0=ALU.mult, op1=ALU.add)
                        op(i)
                    settle()

            def conv_samples(out, src, taps, row, bias, sig=dv):
                old = taps - 1 + T
                for j in range(taps):
                    at = old + NSAMP * j if j < taps - 1 else old - NSAMP
                    dst = smp if j == 0 else smq
                    op(V.tensor_tensor(dst[:], src[:, :, at:at + NSAMP], cols(row + j, NSAMP), ALU.mult))
                    settle()
                    if j:
                        end = j == taps - 1 and bias is None
                        op(V.tensor_tensor(out[:, :, SEQ:T] if end else smp[:], smp[:], smq[:], ALU.add))
                        settle()
                if bias is not None:
                    op(V.tensor_tensor(out[:, :, SEQ:T], smp[:], cols(bias, NSAMP), ALU.add), sig)

            for n in range(LEAD):
                lo(n)
            vec_e.wait_ge(aux_done, AX_H)
            for i in range(C // 2):
                square(i)
            r = v("lru_bx")
            op(V.tensor_scalar(hb[:], vec[:, :, r:r + 4], 0.5, None, ALU.mult))
            r = v("lru_lambda")
            lam = vec[:, :, r:r + LAYERS]
            op(V.scalar_tensor_tensor(out=lam_a[:], in0=lam, scalar=-1.0, in1=lam, op0=ALU.mult, op1=ALU.max), vec_step)
            op(V.tensor_scalar(lam_c[:], lam, -4.0, 0.0, ALU.mult, ALU.max))
            from_scalar()
            op(V.tensor_scalar(lam_d[:], lam_b[:], 2.0, None, ALU.add))
            settle()
            op(V.reciprocal(lam_d[:], lam_d[:]))
            settle()
            op(V.tensor_tensor(lam_b[:], lam_b[:], lam_d[:], ALU.mult))
            settle()
            op(V.tensor_tensor(lam_d[:], lam_b[:], lam_b[:], ALU.mult))
            settle()
            op(V.tensor_scalar(lam_a[:], lam_d[:], 1.0 / 15, None, ALU.mult))
            settle()
            for k in (13, 11, 9, 7, 5, 3):
                op(V.scalar_tensor_tensor(out=lam_a[:], in0=lam_a[:], scalar=1.0 / k, in1=lam_d[:],
                                          op0=ALU.add, op1=ALU.mult))
                settle()
            op(V.scalar_tensor_tensor(out=lam_a[:], in0=lam_a[:], scalar=1.0, in1=lam_b[:], op0=ALU.add, op1=ALU.mult))
            settle()
            op(V.scalar_tensor_tensor(out=sp4[:], in0=lam_a[:], scalar=8.0, in1=lam_c[:], op0=ALU.mult, op1=ALU.add))

            def mixer(l):
                n0 = N_MIX[l]
                norm(v("norm_mix", l))
                for j in range(3):
                    r = v("state_conv_a") + 24 * l + j
                    op(V.tensor_copy(xa[:, :, 3 + T + NSAMP * j:3 + T + NSAMP * (j + 1)], vec[:, :, r:r + 22:3]))
                for j in range(2):
                    r = v("state_conv_b") + 16 * l + j
                    op(V.tensor_copy(ub[:, :, 2 + T + NSAMP * j:2 + T + NSAMP * (j + 1)], vec[:, :, r:r + 15:2]))
                n = n0
                row, bias = v("conv_a_w", 4 * l), v("conv_a_b", l)
                for u in range(SEC):
                    lo(n + u + LEAD)
                    evacuated(n + u)
                    conv(ua, xa, 4, row, bias, u)
                conv_samples(ua, xa, 4, row, bias, ua_ready)
                n += SEC
                for u in range(SEC):
                    s = slice(2 * u, 2 * u + 2)
                    lo(n + u + LEAD)
                    evacuated(n + u)
                    op(V.tensor_tensor(gx[:, s, :], ya[:, s, :], ya[:, s, :], ALU.mult))
                    settle()
                    op(V.tensor_scalar(gx[:, s, :], gx[:, s, :], 0.044715 * GELU_C, GELU_C, ALU.mult, ALU.add))
                    settle()
                    op(V.tensor_tensor(gx[:, s, :], gx[:, s, :], ya[:, s, :], ALU.mult), vec_step if u == SEC - 1 else dv)
                n += SEC
                for u in range(SEC):
                    lo(n + u + LEAD)
                    if u == 2:
                        from_scalar()
                        op(V.scalar_tensor_tensor(out=ya[:], in0=gx, scalar=1.0, in1=ya[:], op0=ALU.add, op1=ALU.mult),
                           vec_step)
                n += SEC
                row = v("conv_b_w", 3 * l)
                for u in range(SEC):
                    s = slice(2 * u, 2 * u + 2)
                    lo(n + u + LEAD)
                    if u == 0:
                        vec_e.wait_ge(aux_done, AX_GATES[l])
                        for c in range(C):
                            op(V.tensor_scalar(gy[:, c, :], gy[:, c, :], 1.0, sp4[:, c, l:l + 1], ALU.add, ALU.mult),
                               vec_step if c == C - 1 else dv)
                    evacuated(n + u)
                    op(V.tensor_tensor(ub[:, s, 2:2 + T], ub[:, s, 2:2 + T], xb[:, s, :], ALU.mult))
                    settle()
                    conv(xb, ub, 3, row, None, u)
                conv_samples(xb, ub, 3, row, None)
                n += SEC
                for u in range(SEC):
                    s = slice(2 * u, 2 * u + 2)
                    lo(n + u + LEAD)
                    if u == 0:
                        from_scalar()
                        op(V.tensor_tensor(gy, gb_f, gb_f, ALU.mult))
                        settle()
                        op(V.scalar_tensor_tensor(out=gy, in0=gy, scalar=1.0, in1=ga_f, op0=ALU.add, op1=ALU.mult),
                           vec_step)
                    evacuated(n + u)
                    op(V.tensor_tensor(xb[:, s, :], xb[:, s, :], ot[:, ots[0] % 2], ALU.mult), ot_free)
                    ots[0] += 1
                n += SEC
                for u in range(SEC):
                    lo(n + u + LEAD)
                    if u == 0:
                        from_scalar()
                        op(V.scalar_tensor_tensor(out=gx, in0=gx, scalar=1.0, in1=gy, op0=ALU.add, op1=ALU.mult))
                        settle()
                    if u == 1:
                        op(V.scalar_tensor_tensor(out=gx, in0=gx, scalar=0.5, in1=ua, op0=ALU.mult, op1=ALU.mult))
                        settle()
                    if u >= 2:
                        for c in range(4 * (u - 2), 4 * (u - 2) + 4):
                            op(V.tensor_tensor_scan(out=ua[:, c, 0:SEQ], data0=gb_f[:, c, 0:SEQ],
                                                    data1=gx[:, c, 0:SEQ], initial=0.0, op0=ALU.mult, op1=ALU.add))
                r = v("state_lru_h") + NSAMP * l
                op(V.tensor_tensor(smp[:], gb_f[:, :, SEQ:T], vec[:, :, r:r + NSAMP], ALU.mult))
                settle()
                op(V.tensor_tensor(ua[:, :, SEQ:T], smp[:], gx[:, :, SEQ:T], ALU.add))
                settle()
                op(V.tensor_copy(st[:, :, 0:11], xa[:, :, SEQ:SEQ + 11]))
                op(V.tensor_copy(st[:, :, 11:21], ub[:, :, SEQ:SEQ + 10]))
                op(V.tensor_copy(st[:, :, 21:30], ua[:, :, SEQ - 1:T]), st_ready)
                n += SEC
                for u in range(SEC):
                    lo(n + u + LEAD)
                    if u == 0:
                        op(V.scalar_tensor_tensor(out=gx, in0=ya[:], scalar=0.5 * XS, in1=ua, op0=ALU.mult, op1=ALU.mult))
                        settle()
                        op(V.tensor_copy(ga[:, 0], gx))
                        settle()
                    s = slice(2 * u, 2 * u + 2)
                    op(V.tensor_tensor(ga[:, 1, s, :], gx[:, s, :], ga[:, 0, s, :], ALU.subtract), ga_ready)
                op(V.tensor_scalar(gb[:, 0], xb[:], XS, None, ALU.mult))
                settle()
                n += SEC
                for u in range(SEC):
                    s = slice(2 * u, 2 * u + 2)
                    op(V.scalar_tensor_tensor(out=gb[:, 1, s, :], in0=xb[:, s, :], scalar=XS, in1=gb[:, 0, s, :],
                                              op0=ALU.mult, op1=ALU.subtract), gb_ready)
                    lo(n + u + LEAD)
                    evacuated(n + u)
                    op(V.scalar_tensor_tensor(out=ya[:, s, :], in0=sa[:, s, :], scalar=1.0, in1=ot[:, ots[0] % 2],
                                              op0=ALU.add, op1=ALU.mult), ot_free)
                    ots[0] += 1
                n += SEC
                for u in range(SEC):
                    s = slice(2 * u, 2 * u + 2)
                    lo(n + u + LEAD)
                    evacuated(n + u)
                    op(V.scalar_tensor_tensor(out=sg[:, s, :], in0=sg[:, s, :], scalar=1.0, in1=ot[:, ots[0] % 2],
                                              op0=ALU.add, op1=ALU.mult), ot_free)
                    ots[0] += 1
                    settle()
                    last = l == 0 and u == SEC - 1
                    op(V.tensor_tensor(ya[:, s, :], ya[:, s, :], sg[:, s, :], ALU.add),
                       pair_free if last else dv, 2 if last else 1)
                    settle()
                    op(V.tensor_scalar(xn[:, 0, s, :], ya[:, s, :], 0.5 * XS, None, ALU.mult))
                    settle()
                    op(V.scalar_tensor_tensor(out=xn[:, 1, s, :], in0=ya[:, s, :], scalar=0.5 * XS, in1=xn[:, 0, s, :],
                                              op0=ALU.mult, op1=ALU.subtract), xm_ready)
                n += SEC
                for u in range(SEC):
                    lo(n + u + LEAD)
                    evacuated(n + u)
                    add_to_h(u)
                    square(u)

            ots = [0]

            def add_to_h(u):
                s = slice(2 * u, 2 * u + 2)
                op(V.tensor_tensor(h[:, s, :], h[:, s, :], ot[:, ots[0] % 2], ALU.add), ot_free)
                ots[0] += 1
                settle()

            def ple(l, n):
                norm(v("norm_ple", l))
                vec_e.wait_ge(aux_done, AX_PLE[l])
                for u in range(SEC):
                    s = slice(2 * u, 2 * u + 2)
                    if n + u + LEAD < N_END:
                        lo(n + u + LEAD)
                    evacuated(n + u)
                    op(V.scalar_tensor_tensor(out=ya[:, s, :], in0=ot[:, ots[0] % 2], scalar=1.0, in1=ya[:, s, :],
                                              op0=ALU.add, op1=ALU.mult), ot_free)
                    ots[0] += 1
                    settle()
                    op(V.scalar_tensor_tensor(out=h[:, s, :], in0=ya[:, s, :], scalar=0.5, in1=h[:, s, :],
                                              op0=ALU.mult, op1=ALU.add))
                    settle()
                    square(u)

            def hidden(p, dst_hi, dst_lo, n=T):
                w, t, g, u = (x[:, p % 2, :, 0:n] for x in (pair_w, pair_t, pair_g, pair_u))
                op(V.scalar_tensor_tensor(out=w, in0=t, scalar=1.0, in1=g, op0=ALU.add, op1=ALU.mult))
                settle()
                op(V.scalar_tensor_tensor(out=w, in0=w, scalar=0.5 * XS, in1=u, op0=ALU.mult, op1=ALU.mult), pair_free)
                settle()
                op(V.tensor_copy(dst_hi, w))
                settle()
                op(V.tensor_tensor(dst_lo, w, dst_hi, ALU.subtract), hid_ready)

            def run_loop(turns, rates, body):
                before = dict(count)
                with vec_e.Fori(0, turns) as it:
                    loop[:] = [it, rates]
                    body(it)
                loop[:] = [None, {}]
                for s, rate in rates.items():
                    assert count[s] - before.get(s, 0) == rate
                    count[s] += rate * (turns - 1)

            mixer(0)
            norm(v("norm_ffn", 0))

            def ffn_turn(it):
                for u in range(SEC):
                    lo(N_GU + u + LEAD, UNIT, it, SEC)
                    if u % 2:
                        evacuated(N_GU + u, it, SEC)
                        at = it * 4 + 2 * (u // 2)
                        hidden(u // 2, hid[:, 0, bass.ds(at, 2), :], hid[:, 1, bass.ds(at, 2), :])

            run_loop(FFN_IT, {lo_done: SEC, dv: 2 * 2, pair_free: 2, hid_ready: 2}, ffn_turn)
            for k in range(3):
                for u in range(SEC):
                    n = N_DN + SEC * k + u
                    lo(n + LEAD)
                    evacuated(n)
                    add_to_h(u)
                    if k == 2:
                        square(u)
            ple(0, N_PLE[0])
            mixer(1)
            norm(v("norm_ffn", 1))

            op(V.memset(ye[0:CAP], 0.0), ys_ready, 2)
            op(V.memset(sel_t[0:CAP, :], 0.0), selt_ready)
            vec_e.wait_ge(aux_done, AX_LOGITS)
            op(V.tensor_reduce(top[:], lg[:], AX.X, ALU.max))
            settle()
            op(V.tensor_tensor(pr[:], lg[:], top[:].unsqueeze(2).to_broadcast([P, 3, NE]), ALU.subtract), vec_step)
            for t in range(3):
                other = lg[:, t, :].unsqueeze(1).to_broadcast([P, NE, NE])
                mine = lg[:, t, :].unsqueeze(2).to_broadcast([P, NE, NE])
                op(V.tensor_tensor(cmp_a[:], other, mine, ALU.is_gt))
                op(V.tensor_tensor(cmp_b[:], other, mine, ALU.is_equal))
                settle()
                op(V.tensor_tensor(cmp_b[:], cmp_b[:], tri[:], ALU.mult))
                settle()
                op(V.tensor_tensor(cmp_a[:], cmp_a[:], cmp_b[:], ALU.add))
                settle()
                op(V.tensor_reduce(rank[:, t, :], cmp_a[:], AX.X, ALU.add))
                settle()
            op(V.tensor_scalar(rank[:], rank[:], 1.5, None, ALU.is_lt), mask_ready)
            settle()
            from_scalar()
            op(V.tensor_tensor(pr[:], pr[:], rank[:], ALU.mult))
            settle()
            op(V.tensor_reduce(den[:], pr[:], AX.X, ALU.add))
            settle()
            op(V.reciprocal(den[:], den[:]))
            settle()
            op(V.tensor_tensor(pr[:], pr[:], den[:].unsqueeze(2).to_broadcast([P, 3, NE]), ALU.mult))
            settle()
            op(V.tensor_scalar(prs[:, :, 0:NE, 0], pr[:], XS, None, ALU.mult))
            settle()
            op(V.scalar_tensor_tensor(out=prs[:, :, 0:NE, 1], in0=pr[:], scalar=XS, in1=prs[:, :, 0:NE, 0],
                                      op0=ALU.mult, op1=ALU.subtract))
            vec_e.wait_ge(aux_done, AX_MASK)
            op(V.tensor_tensor_scan(out=cum, data0=mask_t, data1=mask_t, initial=0.0, op0=ALU.add, op1=ALU.max))
            settle()
            op(V.tensor_scalar(over[:], cum[:, T - 1:T], float(CAP), None, ALU.is_gt))
            settle()
            op(V.tensor_tensor(cum, cum, mask_t, ALU.mult))
            settle()
            op(V.tensor_scalar(cum, cum, -1.0, None, ALU.add), pos_ready)

            def one_hot(e, sig):
                for t in range(3):
                    op(V.tensor_scalar(sel[:, t, :], iota[:], pos[:, t, bass.ds(e, 1)], None, ALU.is_equal))
                op(V.tensor_copy(prs_e[:], prs[:, :, bass.ds(e, 1), :].rearrange("p t e s -> p t (e s)")), sig)

            vec_e.wait_ge(aux_done, AX_POS)
            vec_e.wait_ge(aux_done, AX_PB)
            spilled = vec_e.value_load(flag[0:1, 0:1], min_val=0, max_val=1)
            with vec_e.If(spilled > 0):
                for i, s in enumerate((sp_gu, sp_hid, sp_h, sp_used)):
                    V.memset(spare[:, i:i + 1], 0.0).then_inc(s, 1)
                with vec_e.Fori(0, SPILLS) as p:
                    V.tensor_scalar(pos[:], pos[:], -float(CAP), None, ALU.add)
                    V.tensor_scalar(pb[0:CAP], pb[0:CAP], -float(CAP), None, ALU.add).then_inc(sp_pass, 1)
                    with vec_e.Fori(0, NE) as e:
                        q = p * NE + e
                        vec_e.wait_ge(sp_pass, p + 1)
                        for t in range(3):
                            V.tensor_scalar(sel[:, t, :], iota[:], pos[:, t, bass.ds(e, 1)], None, ALU.is_equal)
                        V.tensor_copy(prs_e[:], prs[:, :, bass.ds(e, 1), :].rearrange("p t e s -> p t (e s)"))
                        V.tensor_scalar(sel_f[0:CAP, :], pb[0:CAP, bass.ds(e, 1), :].rearrange("p e t -> p (e t)"),
                                        slot_id[0:CAP, :], None, ALU.is_equal).then_inc(sp_sel, 1)
                        vec_e.wait_ge(sp_x, q + 1)
                        V.scalar_tensor_tensor(out=csl[0:CAP, :], in0=csr[0:CAP, 0:1], scalar=1.0, in1=csr[0:CAP, 1:2],
                                               op0=ALU.mult, op1=ALU.add).then_inc(sp_csl, 1)
                        with vec_e.Fori(0, EC) as j:
                            vec_e.wait_ge(sp_gu, q * EC + (j + 2))
                            V.scalar_tensor_tensor(out=pair_w[:, 0, 0, 0:CAP], in0=pair_t[:, 0, 0, 0:CAP], scalar=1.0,
                                                   in1=pair_g[:, 0, 0, 0:CAP], op0=ALU.add,
                                                   op1=ALU.mult).then_inc(sp_mm, 1)
                            vec_e.wait_ge(sp_mm, q * EC + (j + 1))
                            dst = hid_f[:, bass.ds(j, 1), :].rearrange("p c t -> p (c t)")
                            V.scalar_tensor_tensor(out=dst, in0=pair_w[:, 0, 0, 0:CAP], scalar=0.5,
                                                   in1=pair_u[:, 0, 0, 0:CAP], op0=ALU.mult,
                                                   op1=ALU.mult).then_inc(sp_hid, 1)
                        with vec_e.Fori(0, C) as j:
                            vec_e.wait_ge(sp_sc, q * C + (j + 1))
                            hc = h[:, bass.ds(j, 1), :].rearrange("p c t -> p (c t)")
                            V.scalar_tensor_tensor(out=hc, in0=acc[:, 3, 0:T], scalar=1.0 / XS, in1=hc,
                                                   op0=ALU.mult, op1=ALU.add).then_inc(sp_h, 1)
                V.tensor_scalar(pos[:], pos[:], float(CAP * SPILLS), None, ALU.add)
                V.tensor_scalar(pb[0:CAP], pb[0:CAP], float(CAP * SPILLS), None, ALU.add).then_inc(sp_pass, 1)
                vec_e.wait_ge(sp_pass, SPILLS + 1)
            with vec_e.Else():
                vec_e.nop()

            def slot_weights():
                op(V.tensor_tensor(csl[0:CAP, :], csr[0:CAP, 0:1], csr[0:CAP, 1:2], ALU.add))
                settle()
                op(V.tensor_scalar(csl[0:CAP, :], csl[0:CAP, :], UNSCALE, None, ALU.mult), csl_ready)

            def add_scattered(c, seen):
                vec_e.wait_ge(sc_full, seen(c + 1))
                op(V.scalar_tensor_tensor(out=h[:, c, :], in0=aux[:, c % 4, 0:T], scalar=1.0 / XS, in1=h[:, c, :],
                                          op0=ALU.mult, op1=ALU.add), sc_done)

            op(V.memset(spare[:, 4:5], 0.0), sc_done, 8)
            one_hot(0, sel_ready)
            vec_e.wait_ge(gat_done, 4)
            slot_weights()

            def expert(e):
                for u in range(MOE_U):
                    n = N_MOE + u
                    lo(n + LEAD, moe_unit_size(u + LEAD), e, MOE_U)
                    if u in (2, 3, 5, 7):
                        c = 2 * (2, 3, 5, 7).index(u)
                        add_scattered(c, lambda i: e * 8 + i)
                        add_scattered(c + 1, lambda i: e * 8 + i)
                    if u < MOE_GU and u % 2:
                        p = u // 2
                        vec_e.wait_ge(evac_done, e * MOE_EVAC + (n + 1))
                        hidden(p, hid_e[:, 0, 2 * p:2 * p + 2, :], hid_e[:, 1, 2 * p:2 * p + 2, :], CAP)
                    if u == 9:
                        op(V.tensor_scalar(sel_t[0:CAP, :], pb[0:CAP, bass.ds(e, 1), :].rearrange("p e t -> p (e t)"),
                                           slot_id[0:CAP, :], None, ALU.is_equal), selt_ready)
                    if u == 7:
                        one_hot(e + 1, sel_ready)
                    if u in (MOE_GU + 5, MOE_U - 1):
                        half = (u - MOE_GU) // 6
                        vec_e.wait_ge(evac_done, e * MOE_EVAC + (N_MOE + MOE_GU + half + 1))
                        s = slice(half * 512, (half + 1) * 512)
                        op(V.scalar_tensor_tensor(out=ye[0:CAP, 1, s], in0=acc[0:CAP, 2 + half, :],
                                                  scalar=csl[0:CAP, :], in1=ye[0:CAP, 0, s],
                                                  op0=ALU.mult, op1=ALU.subtract), ys_ready)
                settle()
                vec_e.wait_ge(gat_done, e * 4 + 8)
                slot_weights()

            run_loop(NE, {lo_done: MOE_U, dv: 2 * 6 + 3 + 1, pair_free: 6, hid_ready: 6, ys_ready: 2, sc_done: 8,
                          selt_ready: 1, sel_ready: 1, csl_ready: 1}, expert)
            for c in range(C):
                add_scattered(c, lambda i: NE * 8 + i)
                if c % 2:
                    settle()
                    square(c // 2)
            ple(1, N_PLE[1])
            norm(v("final_norm"), split=False)


_INS = ["x_prompt", "x_sample", "state_lru_h", "state_conv_a", "state_conv_b", "p_prompt", "p_sample", "norm_mix",
        "w_in", "conv_a_w", "conv_a_b", "lru_wx", "lru_bx", "lru_wa", "lru_ba", "lru_lambda", "w_a_out", "conv_b_w",
        "w_b_out", "w_o", "norm_ffn", "ffn_w_gu", "ffn_w_dn", "router", "moe_w_gu", "moe_w_dn", "norm_ple",
        "w_ple_gate", "w_ple_proj", "final_norm"]
_OUTS = [("y_prompt", (1, SEQ, D)), ("y_sample", (NSAMP, 1, D)), ("lru_h_prompt", (LAYERS, 1, D)),
         ("conv_a_prompt", (LAYERS, 1, 3, D)), ("conv_b_prompt", (LAYERS, 1, 2, D)),
         ("lru_h_sample", (LAYERS, NSAMP, D)), ("conv_a_sample", (LAYERS, NSAMP, 3, D)),
         ("conv_b_sample", (LAYERS, NSAMP, 2, D))]


def kernel(**inputs):
    import numpy as np
    import concourse.bacc as bacc
    from concourse.bass_utils import run_bass_kernel_spmd

    nc = bacc.Bacc("TRN2", target_bir_lowering=False, num_devices=1)
    arrays, ins, outs = {}, {}, {}
    for name in _INS:
        x = np.ascontiguousarray(inputs[name])
        arrays[f"in_{name}"] = x
        ins[name] = nc.dram_tensor(f"in_{name}", x.shape, mybir.dt.from_np(x.dtype), kind="ExternalInput").ap()
    for name, shape in _OUTS:
        outs[name] = nc.dram_tensor(f"out_{name}", shape, F32, kind="ExternalOutput").ap()
    program(nc, ins, outs)
    r = run_bass_kernel_spmd(nc, [arrays], core_ids=[0])
    return tuple(r.results[0][f"out_{name}"] for name, _ in _OUTS)
```

```python
import math
from contextlib import ExitStack

import concourse.bass as bass
from concourse import mybir

F32 = mybir.dt.float32
F16 = mybir.dt.float16
ALU = mybir.AluOpType
ACT = mybir.ActivationFunctionType
AX = mybir.AxisListType

P = 128
SEQ, NSAMP, D, LAYERS = 256, 8, 1024, 2
T = SEQ + NSAMP
C = D // P
HEADS, HB = 16, 64
PLE, PC = 256, 2
FF, FE, NE = 3072, 1536, 8
EPS = 1e-6

WS, XS = 256.0, 16.0
UNSCALE = 1.0 / (WS * XS)

SLOTS = 4
MOE_SLOTS = SLOTS + 1
UNIT = 2048
LEAD = SLOTS - 1

SEC = 4
FFN_IT, MOE_GU, MOE_DN = FF // 512, 2 * FE // 256, 8
EC = FE // P
DN_K = EC // 4
CAP = 96
SPILLS = -(-T // CAP) - 1
TOK = ((0, P), (P, P), (SEQ, NSAMP))
MOE_U = MOE_GU + MOE_DN

IN_SECTIONS = 7
MIX_U = (IN_SECTIONS + 3) * SEC
N_MIX = [0, MIX_U + (FFN_IT + 3) * SEC + SEC]
N_GU = N_MIX[0] + MIX_U
N_DN = N_GU + FFN_IT * SEC
N_MOE = N_MIX[1] + MIX_U
N_PLE = [N_DN + 3 * SEC, N_MOE + NE * MOE_U]
MOE_EVAC = MOE_GU + 2
UNCOUNTED = NE * (MOE_U - MOE_EVAC)
N_END = N_PLE[1] + SEC

IN_RUNS = [(1, 2, 1), (3, 1, 4), (4, 1, 3), (5, 2, 5)]

GELU_C = math.sqrt(2.0 / math.pi)
A_EXT = 3 + T + 24
B_EXT = 2 + T + 16


def row_table():
    at, out = 0, {}
    for name, n in (("norm_mix", 2), ("conv_a_w", 8), ("conv_a_b", 2), ("lru_bx", 2), ("lru_ba", 2),
                    ("lru_lambda", 2), ("conv_b_w", 6), ("norm_ffn", 2), ("norm_ple", 2), ("final_norm", 1),
                    ("state_lru_h", 16), ("state_conv_a", 48), ("state_conv_b", 32)):
        out[name] = (at, n)
        at += n
    return out, at


ROWS, N_ROWS = row_table()


def raw_turn(n):
    if n < N_MOE:
        return n % SLOTS, n // SLOTS + 1
    if n < N_PLE[1]:
        u = n - N_MOE
        return u % MOE_SLOTS, u // MOE_SLOTS + 1 + (N_MOE // SLOTS if u % MOE_SLOTS < SLOTS else 0)
    return (n - N_PLE[1]) % SLOTS, N_MOE // SLOTS + NE * MOE_U // MOE_SLOTS + 1


def moe_unit_size(u):
    return UNIT if u % MOE_U < MOE_GU else DN_K * 512


def program(nc, a, o):
    ctx = ExitStack()
    with ctx:
        def sb(name, shape, dt=F32):
            return ctx.enter_context(nc.sbuf_tensor(name, shape, dt))

        def sem(name):
            return ctx.enter_context(nc.semaphore(name))
        raw = sb("raw", [P, SLOTS, UNIT])
        wh = sb("wh", [P, SLOTS, UNIT], F16)
        wl = sb("wl", [P, SLOTS, UNIT], F16)
        h = sb("h", [P, C, T])
        xa = sb("xa", [P, C, A_EXT])
        ub = sb("ub", [P, C, B_EXT])
        ya = sb("ya", [P, C, T])
        xb = sb("xb", [P, C, T])
        sa = sb("sa", [P, C, T])
        sg = sb("sg", [P, C, T])
        w1 = sb("w1", [P, 3, C, T])
        xn = sb("xn", [P, 2, C, T], F16)
        ga = sb("ga", [P, 2, C, T], F16)
        gb = sb("gb", [P, 2, C, T], F16)
        side = sb("side", [P, 2, C, P])
        vec = sb("vec", [P, C, P])
        pt = sb("pt", [P, LAYERS, PC, T])
        ot = sb("ot", [P, 2, 2, T])
        var = sb("var", [P, T])
        std = sb("std", [P, T])
        rstd = sb("rstd", [P, T])
        rtmp = sb("rtmp", [P, T])
        ident = sb("ident", [P, P])
        ones = sb("ones", [P, P])
        tri = sb("tri", [P, NE, NE])
        eps = sb("eps", [P, 1])
        root = sb("root", [P, 1])
        tiny = sb("tiny", [P, 1])
        hb = sb("hb", [P, C, 4])
        sp4 = sb("sp4", [P, C, LAYERS])
        lam_a = sb("lam_a", [P, C, LAYERS])
        lam_b = sb("lam_b", [P, C, LAYERS])
        lam_c = sb("lam_c", [P, C, LAYERS])
        lam_d = sb("lam_d", [P, C, LAYERS])
        smp = sb("smp", [P, C, NSAMP])
        smq = sb("smq", [P, C, NSAMP])
        st = sb("st", [P, C, 30])
        rows = sb("rows", [32, D])
        rt = sb("rt", [P, C, NE])
        lg = sb("lg", [P, 3, NE])
        prs = sb("prs", [P, 3, NE + 1, 2], F16)
        prs_e = sb("prs_e", [P, 3, 2], F16)
        iota = sb("iota", [P, CAP])
        lgt = sb("lgt", [NE, T])
        pos = sb("pos", [P, 3, NE + 1])
        over = sb("over", [NE, 1])
        flag = sb("flag", [1, 1], mybir.dt.int32)
        spare = sb("spare", [1, 5])
        csr = sb("csr", [P, 2])
        csl = sb("csl", [P, 1])
        identh = sb("identh", [P, P], F16)
        rank = sb("rank", [P, 3, NE])
        top = sb("top", [P, 3])
        den = sb("den", [P, 3])
        pr = sb("pr", [P, 3, NE])

        nf = xb
        raw_slot = [raw[:, i] for i in range(SLOTS)] + [xb[:].rearrange("p c t -> p (c t)")[:, 0:UNIT]]
        sq = sa
        ua, gx, gy = w1[:, 0], w1[:, 1], w1[:, 2]
        ga_f = ga[:].rearrange("p a c t -> p (a c t)").bitcast(F32).rearrange("p (c t) -> p c t", c=C)
        gb_f = gb[:].rearrange("p a c t -> p (a c t)").bitcast(F32).rearrange("p (c t) -> p c t", c=C)
        hid = w1[:].rearrange("p a c t -> p (a c t)").bitcast(F16).rearrange("p (s c t) -> p s c t", s=2, c=24)
        w1_flat = w1[:].rearrange("p a c t -> p (a c t)")
        vrows = w1_flat[:, 0:D]
        xrows = w1_flat[:, D:D + 3 * D].rearrange("p (t n) -> p t n", t=3)
        prows = w1_flat[:, 4 * D:4 * D + 3 * LAYERS * PLE].rearrange("p (l t n) -> p l t n", l=LAYERS, t=3)
        yrows = w1_flat[:, 0:3 * D].rearrange("p (t n) -> p t n", t=3)
        w1_half = w1_flat.bitcast(F16)
        hid_e = w1_half[:, 0:2 * EC * CAP].rearrange("p (s c t) -> p s c t", s=2, c=EC)
        at = 2 * EC * CAP
        nt = w1_half[:, at:at + 6 * D].rearrange("p (s t n) -> p s t n", s=2, t=3)
        at = (at + 6 * D) // 2
        sel_f = w1_flat[:, at:at + T]
        xg = ga[:].rearrange("p a c t -> p (a c t)")[:, 0:2 * C * CAP].rearrange("p (s c t) -> p s c t", s=2, c=C)
        sel = ga[:].rearrange("p a c t -> p (a c t)")[:, 2 * C * CAP:2 * C * CAP + 3 * CAP].rearrange("p (t n) -> p t n", t=3)
        ye = gb[:].rearrange("p a c t -> p (a c t)")[:, 0:2 * D].rearrange("p (s n) -> p s n", s=2)
        sel_t = gb[:].rearrange("p a c t -> p (a c t)")[:, 2 * D:2 * D + T]
        mask_t, cum = var[0:NE, :], rtmp[0:NE, :]
        cmp_a, cmp_b = (x[:, 0:3 * NE * NE].rearrange("p (t m o) -> p t m o", t=3, m=NE) for x in (std, rstd))
        ow = xa[:].rearrange("p c t -> p (c t)")[:, 0:UNIT]
        ub_flat = ub[:].rearrange("p c t -> p (c t)")
        xg_f = ub_flat[:, 0:C * CAP].rearrange("p (c t) -> p c t", c=C)
        hid_f = ub_flat[:, C * CAP:(C + EC) * CAP].rearrange("p (c t) -> p c t", c=EC)
        y_f = ub_flat[:, (C + EC) * CAP:(C + EC) * CAP + P]
        pair = sa[:].rearrange("p (k s c) t -> p k s c t", k=2, s=2)
        pair_g, pair_t = pair[:, 0], pair[:, 1]
        pair2 = sg[:].rearrange("p (k s c) t -> p k s c t", k=2, s=2)
        pair_u, pair_w = pair2[:, 0], pair2[:, 1]
        plew = side[:].rearrange("p a c n -> p (a c n)").rearrange("p (k n) -> p k n", k=PC)

        acc = ctx.enter_context(nc.psum_tensor("acc", [P, 4, 512], F32))
        aux = ctx.enter_context(nc.psum_tensor("aux", [P, 4, 512], F32))

        w_loaded = [sem(f"w_loaded{i}") for i in range(MOE_SLOTS)]
        hi_done, lo_done = sem("hi_done"), sem("lo_done")
        unit_mm = sem("unit_mm")
        evac_done = sem("evac_done")
        aux_full, aux_done = sem("aux_full"), sem("aux_done")
        ot_free, pair_free = sem("ot_free"), sem("pair_free")
        dv = sem("dv")
        vec_step, act_step = sem("vec_step"), sem("act_step")
        const_ready = sem("const_ready")
        small_loaded, x_loaded, p_loaded = sem("small_loaded"), sem("x_loaded"), sem("p_loaded")
        side_loaded = sem("side_loaded")
        sq_ready = sem("sq_ready")
        tile_mm, tile_out = sem("tile_mm"), sem("tile_out")
        nf_ready, nh_ready, xn_ready = sem("nf_ready"), sem("nh_ready"), sem("xn_ready")
        ua_ready = sem("ua_ready")
        ga_ready, gb_ready, xm_ready = sem("ga_ready"), sem("gb_ready"), sem("xm_ready")
        st_ready, rows_out = sem("st_ready"), sem("rows_out")
        hid_ready = sem("hid_ready")
        mask_ready, pos_ready = sem("mask_ready"), sem("pos_ready")
        sel_ready, selt_ready = sem("sel_ready"), sem("selt_ready")
        gat_full, gat_done = sem("gat_full"), sem("gat_done")
        sc_full, sc_done = sem("sc_full"), sem("sc_done")
        csl_ready = sem("csl_ready")
        ys_ready = sem("ys_ready")
        selt_full = sem("selt_full")
        sp_sel, sp_gat, sp_x, sp_csl = sem("sp_sel"), sem("sp_gat"), sem("sp_x"), sem("sp_csl")
        sp_w, sp_used = sem("sp_w"), sem("sp_used")
        sp_mm, sp_gu, sp_hid = sem("sp_mm"), sem("sp_gu"), sem("sp_hid")
        sp_ye, sp_sc, sp_h, sp_pass = sem("sp_ye"), sem("sp_sc"), sem("sp_h"), sem("sp_pass")
        y_out, old_out = sem("y_out"), sem("old_out")

        def v(name, layer=0, k=0):
            return ROWS[name][0] + layer + k

        N_FIRST = 5
        N_CONST = 13 + NE

        AX_H = C
        AX_VEC = AX_H + 1 + 2
        AX_P = AX_VEC + LAYERS * PC
        AX_NORM, AX_GATES, AX_STATES, AX_PLE = [], [], [], []
        at = AX_H
        for l in range(LAYERS):
            AX_NORM.append(at + 1)
            AX_GATES.append((AX_NORM[-1] if l else AX_P) + 2 * C)
            AX_STATES.append(AX_GATES[-1] + 2)
            AX_NORM.append(AX_STATES[-1] + 1)
            at = AX_NORM[-1]
            if l == 1:
                AX_LGT = at + 1
                AX_LOGITS = AX_LGT + 1
                AX_MASK = AX_LOGITS + 3 + 1
                AX_POS = AX_MASK + 1
                AX_ROUTED = at = AX_POS + 3
            AX_NORM.append(at + 1)
            AX_PLE.append(AX_NORM[-1] + C)
            at = AX_PLE[-1]
        AX_NORM.append(at + 1)
        AX_OUT = AX_NORM[-1]

        block = ctx.enter_context(nc.Block())

        @block.sync
        def _(sp):
            sp.dma_start(xrows[:, 0, :], a["x_prompt"][0, 0:P, :]).then_inc(x_loaded, 16)
            sp.dma_start(xrows[:, 1, :], a["x_prompt"][0, P:2 * P, :]).then_inc(x_loaded, 16)
            sp.dma_start(xrows[0:NSAMP, 2, :], a["x_sample"][:, 0, :]).then_inc(x_loaded, 16)

            def small_rows():
                small = [(name, a[name]) for name in ROWS]
                for name, ap in small:
                    r, n = ROWS[name]
                    if len(ap.shape) == 1:
                        src = ap.rearrange("(a n) -> a n", a=1)
                    elif len(ap.shape) == 2:
                        src = ap
                    elif len(ap.shape) == 3:
                        src = ap.rearrange("a b n -> (a b) n")
                    else:
                        src = ap.rearrange("a b c n -> (a b c) n")
                    sp.dma_start(vrows[r:r + n, :], src).then_inc(small_loaded, 16)

            def load(n, src, slot, k, it=None, step=0, slots=SLOTS):
                cols = src.shape[-1]
                if it is not None:
                    sp.wait_ge(hi_done, it * step + (n + 1 - slots))
                    sp.wait_ge(lo_done, it * step + (n + 1 - slots))
                elif n >= SLOTS:
                    sp.wait_ge(hi_done, n - LEAD)
                    sp.wait_ge(lo_done, n - LEAD)
                dst = raw_slot[slot][:, 0:k * cols].rearrange("p (c m) -> p c m", c=k)
                sp.dma_start(dst, src).then_inc(w_loaded[slot], 16)

            def matrix(w, n, k0=0):
                v_ = w.rearrange("(c p) m -> p c m", p=P)
                for u in range(SEC):
                    if n + u == 1:
                        small_rows()
                    load(n + u, v_[:, k0:k0 + C, u * 256:(u + 1) * 256], u, C)

            def mixer(l):
                w = a["w_in"][l]
                by_section = w.rearrange("(c p) (s m) -> p c s m", p=P, s=IN_SECTIONS)
                n = N_MIX[l]
                matrix(w[:, 0:D], n)
                for first, count, col in IN_RUNS:
                    with sp.Fori(0, count) as s:
                        for u in range(SEC):
                            src = by_section[:, :, bass.ds(s + col, 1), u * 256:(u + 1) * 256]
                            load(n + SEC * first + u, src.rearrange("p c s m -> p c (s m)"), u, C, s, SEC)
                matrix(a["w_a_out"][l], N_MIX[l] + 28)
                matrix(a["w_b_out"][l], N_MIX[l] + 32)
                matrix(a["w_o"][l], N_MIX[l] + 36)

            mixer(0)
            gu = a["ffn_w_gu"][0].rearrange("(c p) (g i m) -> p c g i m", p=P, g=2, i=FFN_IT)
            with sp.Fori(0, FFN_IT) as it:
                for u in range(SEC):
                    g, half = u % 2, u // 2
                    src = gu[:, :, g, bass.ds(it, 1), half * 256:(half + 1) * 256].rearrange("p c i m -> p c (i m)")
                    load(N_GU + u, src, u, C, it, SEC)
            dn = a["ffn_w_dn"][0].rearrange("(g c p) m -> p g c m", p=P, g=3)
            with sp.Fori(0, 3) as it:
                for u in range(SEC):
                    src = dn[:, bass.ds(it, 1), :, u * 256:(u + 1) * 256].rearrange("p g c m -> p (g c) m")
                    load(N_DN + u, src, u, C, it, SEC)
            matrix(a["w_ple_gate"][0], N_PLE[0])
            mixer(1)
            n0 = N_MOE
            gu = a["moe_w_gu"][0].rearrange("e (c p) m -> p e c m", p=P)
            dn = a["moe_w_dn"][0].rearrange("e (c p) m -> p e c m", p=P)
            sp.wait_ge(hi_done, N_MOE)
            sp.wait_ge(lo_done, N_MOE)
            with sp.Fori(0, NE) as e:
                for u in range(MOE_GU):
                    if u == SLOTS:
                        sp.wait_ge(aux_full, AX_LGT)
                        sp.wait_ge(xn_ready, 4 * 5)
                    col = (u % 2) * FE + (u // 2) * 256
                    load(n0 + u, gu[:, bass.ds(e, 1), :, col:col + 256].rearrange("p e c m -> p (e c) m"),
                         u % MOE_SLOTS, C, e, MOE_U, MOE_SLOTS)
                for u in range(MOE_DN):
                    half, k = u // 4, u % 4 * DN_K
                    src = dn[:, bass.ds(e, 1), k:k + DN_K, half * 512:(half + 1) * 512]
                    load(n0 + MOE_GU + u, src.rearrange("p e c m -> p (e c) m"), (MOE_GU + u) % MOE_SLOTS, DN_K, e,
                         MOE_U, MOE_SLOTS)
            matrix(a["w_ple_gate"][1], N_PLE[1])

            for g in range(2):
                cols = slice(g * 512, (g + 1) * 512)
                for t, dst in enumerate((o["y_prompt"][0, 0:P, cols], o["y_prompt"][0, P:2 * P, cols],
                                         o["y_sample"][:, 0, cols])):
                    sp.wait_ge(aux_done, AX_OUT + 3 * g + t + 1)
                    sp.dma_start(dst, yrows[0:TOK[t][1], t, cols]).then_inc(y_out, 16)
            sp.wait_ge(y_out, 16 * 6)

        @block.gpsimd
        def _(pool):
            nc.gpsimd.memset(ident[:], 0.0).then_inc(const_ready, 1)
            pool.wait_ge(const_ready, 1)
            nc.gpsimd.affine_select(out=ident[:], in_=ident[:], compare_op=ALU.not_equal, fill=1.0, base=0,
                                    pattern=[[-1, P]], channel_multiplier=1).then_inc(const_ready, 1)
            nc.gpsimd.memset(ones[:], 1.0).then_inc(const_ready, 1)
            nc.gpsimd.memset(eps[:], EPS).then_inc(const_ready, 1)
            pool.wait_ge(const_ready, 2)
            nc.gpsimd.tensor_copy(identh[:], ident[:]).then_inc(const_ready, 1)
            nc.gpsimd.memset(tiny[:], 1e-30).then_inc(const_ready, 1)
            nc.gpsimd.memset(xa[:, :, 0:3], 0.0).then_inc(const_ready, 1)
            nc.gpsimd.memset(ub[:, :, 0:2], 0.0).then_inc(const_ready, 1)
            nc.gpsimd.memset(lg[:], 0.0).then_inc(const_ready, 1)
            nc.gpsimd.memset(pos[:], -1.0).then_inc(const_ready, 1)
            nc.gpsimd.memset(prs[:], 0.0).then_inc(const_ready, 1)
            nc.gpsimd.iota(iota[:], pattern=[[1, CAP]], base=0, channel_multiplier=0,
                           allow_small_or_imprecise_dtypes=True).then_inc(const_ready, 1)
            nc.gpsimd.memset(tri[:], 0.0).then_inc(const_ready, 1)
            nc.gpsimd.memset(side[:], 0.0).then_inc(const_ready, 1)
            pool.wait_ge(const_ready, 14)
            for e in range(1, NE):
                nc.gpsimd.memset(tri[:, e, 0:e], 1.0).then_inc(const_ready, 1)

            def side_gates(l):
                for g, w in enumerate((a["lru_wx"], a["lru_wa"])):
                    heads = w[l].rearrange("(c two) i j -> two i c j", two=2)
                    for k in range(2):
                        at = k * HB
                        pool.dma_start(side[at:at + HB, g, :, at:at + HB], heads[k]).then_inc(side_loaded, 16)

            for l in range(LAYERS):
                pool.dma_start(prows[:, l, 0, :], a["p_prompt"][l, 0, 0:P, :]).then_inc(p_loaded, 16)
                pool.dma_start(prows[:, l, 1, :], a["p_prompt"][l, 0, P:2 * P, :]).then_inc(p_loaded, 16)
                pool.dma_start(prows[0:NSAMP, l, 2, :], a["p_sample"][l, :, 0, :]).then_inc(p_loaded, 16)
            pool.dma_start(rt[:], a["router"][0].rearrange("(c p) e -> p c e", p=P)).then_inc(p_loaded, 16)

            side_gates(0)
            for l in range(LAYERS):
                pool.dma_start(o["conv_a_sample"][l, :, 0:2, :], a["state_conv_a"][l, :, 1:3, :]).then_inc(old_out, 16)
                pool.dma_start(o["conv_b_sample"][l, :, 0:1, :], a["state_conv_b"][l, :, 1:2, :]).then_inc(old_out, 16)
            for l in range(LAYERS):
                pool.wait_ge(aux_full, AX_GATES[l])
                pool.dma_start(plew, a["w_ple_proj"][l].rearrange("(k p) n -> p k n", p=P)).then_inc(side_loaded, 16)
                pool.wait_ge(aux_done, AX_STATES[l])
                for dst, r, n in ((o["conv_a_prompt"][l, 0], 0, 3), (o["conv_a_sample"][l, :, 2, :], 3, NSAMP),
                                  (o["conv_b_prompt"][l, 0], 11, 2), (o["conv_b_sample"][l, :, 1, :], 13, NSAMP),
                                  (o["lru_h_prompt"][l], 21, 1), (o["lru_h_sample"][l], 22, NSAMP)):
                    pool.dma_start(dst, rows[r:r + n, :]).then_inc(rows_out, 16)
                if l + 1 < LAYERS:
                    pool.wait_ge(aux_full, AX_PLE[l])
                    nc.gpsimd.memset(side[:], 0.0).then_inc(const_ready, 1)
                    pool.wait_ge(const_ready, N_CONST + 1)
                    side_gates(l + 1)
            pool.wait_ge(aux_done, AX_POS)
            spilled = pool.value_load(flag[0:1, 0:1], min_val=0, max_val=1)
            gu = a["moe_w_gu"][0].rearrange("e (c p) (g j m) -> p e g j c m", p=P, g=2, j=EC)
            dn = a["moe_w_dn"][0].rearrange("e (c p) (j m) -> p e j c m", p=P, j=C)
            with pool.If(spilled > 0):
                with pool.Fori(0, SPILLS) as p:
                    with pool.Fori(0, NE) as e:
                        with pool.Fori(0, EC) as j:
                            pool.wait_ge(sp_used, (p * NE + e) * (EC + C) + (j + 1))
                            for g in range(2):
                                src = gu[:, bass.ds(e, 1), g, bass.ds(j, 1), :, :]
                                pool.dma_start(ow[:, g * 1024:(g + 1) * 1024].rearrange("p (c m) -> p c m", c=C),
                                               src.rearrange("p e j c m -> p (e j c) m")).then_inc(sp_w, 16)
                        with pool.Fori(0, C) as j:
                            pool.wait_ge(sp_used, (p * NE + e) * (EC + C) + (j + (EC + 1)))
                            src = dn[:, bass.ds(e, 1), bass.ds(j, 1), :, :]
                            for g in range(2):
                                c = EC // 2
                                pool.dma_start(ow[:, g * c * P:(g + 1) * c * P].rearrange("p (c m) -> p c m", c=c),
                                               src[:, :, :, g * c:(g + 1) * c].rearrange("p e j c m -> p (e j c) m")
                                               ).then_inc(sp_w, 16)
            with pool.Else():
                pool.nop()
            pool.wait_ge(rows_out, 16 * 6 * LAYERS)
            pool.wait_ge(old_out, 32 * LAYERS)

        @block.tensor
        def _(pe):
            ax = [0]

            def aux_bank():
                i = ax[0]
                ax[0] += 1
                if i >= 4:
                    pe.wait_ge(aux_done, i - 3)
                return aux[:, i % 4, :]

            def unit(n, slot, half, x, k_chunks, cols, x0=0, at=None, it=None, step=0,
                     last_unit=False):
                extra = 0 if it is None else it * step
                if it is not None:
                    pe.wait_ge(evac_done, extra + (n - 1))
                    pe.wait_ge(hi_done, extra + (n + 1))
                    pe.wait_ge(lo_done, extra + (n + 1))
                else:
                    if n >= 2:
                        pe.wait_ge(evac_done, n - 1 - (UNCOUNTED if n >= N_PLE[1] else 0))
                    pe.wait_ge(hi_done, n + 1)
                    pe.wait_ge(lo_done, n + 1)
                th = wh[:, slot, 0:k_chunks * cols].rearrange("p (c m) -> p c m", c=k_chunks)
                tl = wl[:, slot, 0:k_chunks * cols].rearrange("p (c m) -> p c m", c=k_chunks)
                if at:
                    for k in range(k_chunks):
                        if k in at:
                            pe.wait_ge(*at[k][0])
                        for m in range(2):
                            bank = acc[:, 2 * half + m, 0:T]
                            hi, lo = th[:, k, m * P:(m + 1) * P], tl[:, k, m * P:(m + 1) * P]
                            nc.tensor.matmul(bank, hi, x[:, 0, x0 + k, :], start=(k == 0), stop=False)
                            nc.tensor.matmul(bank, lo, x[:, 0, x0 + k, :], start=False, stop=False)
                        if k % 2:
                            if k - 1 in at:
                                pe.wait_ge(*at[k - 1][-1])
                            for j in (k - 1, k):
                                for m in range(2):
                                    last = nc.tensor.matmul(acc[:, 2 * half + m, 0:T], th[:, j, m * P:(m + 1) * P],
                                                            x[:, 1, x0 + j, :], start=False, stop=(j == k_chunks - 1))
                    last.then_inc(unit_mm, 1)
                    return
                for m in range(cols // P):
                    bank = acc[:, 2 * half + m, 0:T]
                    for k in range(k_chunks):
                        hi, lo = th[:, k, m * P:(m + 1) * P], tl[:, k, m * P:(m + 1) * P]
                        nc.tensor.matmul(bank, hi, x[:, 0, x0 + k, :], start=(k == 0), stop=False)
                        nc.tensor.matmul(bank, hi, x[:, 1, x0 + k, :], start=False, stop=False)
                        last = nc.tensor.matmul(bank, lo, x[:, 0, x0 + k, :], start=False, stop=(k == k_chunks - 1))
                    if last_unit and m == 0:
                        last.then_inc(tile_mm, 1)
                last.then_inc(unit_mm, 1)

            def matrix(n, x, ready=None, base=0, before_norm=False):
                at = None
                if ready is not None:
                    at = {2 * i: [(ready, base + i + 1)] for i in range(C // 2)}
                if ready is xn_ready:
                    for i in range(C // 2):
                        at[2 * i].insert(0, (nh_ready, base + i + 1))
                for u in range(SEC):
                    unit(n + u, u, u % 2, x, C, 256, at=at if u == 0 else None, last_unit=before_norm and u == SEC - 1)

            def sections(n, count, x):
                with pe.Fori(0, count) as s:
                    for u in range(SEC):
                        unit(n + u, u, u % 2, x, C, 256, it=s, step=SEC)

            def keep_warm(n):
                for _ in range(n):
                    nc.tensor.matmul(acc[:, 0, :], identh[:], identh[:, 0:1].to_broadcast([P, 512]), start=True,
                                     stop=True)

            norms = [0]

            def norm_stats():
                k = norms[0]
                norms[0] += 1
                bank = aux_bank()
                for c in (0, 1, C - 2, C - 1):
                    if c != 1:
                        pe.wait_ge(sq_ready, 3 * k + max(c - C + 4, 1))
                    last = nc.tensor.matmul(bank[:, 0:T], ones[:], sq[:, c, :], start=(c == 0), stop=(c == C - 1))
                last.then_inc(aux_full, 1)
                if k % 3 < 2:
                    keep_warm(18 if k < 3 * LAYERS else 26)

            def columns(bank, src, c):
                nc.tensor.transpose(bank[:, 0:P], src[:, 0, c * P:(c + 1) * P], ident[:])
                nc.tensor.transpose(bank[:, P:2 * P], src[:, 1, c * P:(c + 1) * P], ident[:])
                return nc.tensor.transpose(bank[:, SEQ:T], src[0:NSAMP, 2, c * P:(c + 1) * P], ident[0:NSAMP, 0:NSAMP])

            def small_rows():
                pe.wait_ge(const_ready, N_CONST)
                pe.wait_ge(small_loaded, 16 * len(ROWS))
                for g in range(2):
                    bank = aux_bank()
                    for c in range(4):
                        at = (4 * g + c) * P
                        last = nc.tensor.transpose(bank[:, c * P:c * P + N_ROWS], vrows[0:N_ROWS, at:at + P],
                                                   ident[0:N_ROWS, 0:N_ROWS])
                    last.then_inc(aux_full, 1)

            def embeddings():
                pe.wait_ge(p_loaded, 16 * (3 * LAYERS + 1))
                for l in range(LAYERS):
                    for c in range(PC):
                        columns(aux_bank(), prows[:, l], c).then_inc(aux_full, 1)

            pe.wait_ge(const_ready, N_FIRST)
            keep_warm(8)
            pe.wait_ge(x_loaded, 48)
            for c in range(C):
                columns(aux_bank(), xrows, c).then_inc(aux_full, 1)

            def mixer(l):
                n0 = N_MIX[l]
                norm_stats()
                if l == 0:
                    small_rows()
                matrix(n0, xn, xn_ready, 4 * 3 * l)
                if l == 0:
                    embeddings()
                sections(n0 + SEC, 2, xn)
                pe.wait_ge(ua_ready, l + 1)
                pe.wait_ge(side_loaded, 16 * (5 * l + 4))
                for g in range(2):
                    for c in range(C):
                        last = nc.tensor.matmul(aux_bank()[:, 0:T], side[:, g, c, :], ua[:, c, :], start=True, stop=True)
                        last.then_inc(aux_full, 1)
                sections(n0 + 3 * SEC, 4, xn)
                pe.wait_ge(st_ready, l + 1)
                for g in range(2):
                    bank = aux_bank()
                    for c in range(4):
                        last = nc.tensor.transpose(bank[0:30, c * P:(c + 1) * P], st[:, 4 * g + c, :], ident[:])
                    last.then_inc(aux_full, 1)
                matrix(n0 + 28, ga, ga_ready, 4 * l)
                matrix(n0 + 32, gb, gb_ready, 4 * l)
                matrix(n0 + 36, xn, xm_ready, 4 * l, before_norm=True)

            def ple(l, n):
                norm_stats()
                pe.wait_ge(side_loaded, 16 * 5 * (l + 1))
                if l:
                    pe.wait_ge(sc_done, 8 * NE + 16)
                for m in range(C):
                    bank = aux_bank()
                    for k in range(PC):
                        last = nc.tensor.matmul(bank[:, 0:T], plew[:, k, m * P:(m + 1) * P], pt[:, l, k, :],
                                                start=(k == 0), stop=(k == PC - 1))
                    last.then_inc(aux_full, 1)
                matrix(n, xn, xn_ready, 4 * (3 * l + 2), before_norm=True)

            mixer(0)
            norm_stats()
            matrix(N_GU, xn, xn_ready, 4)
            sections(N_GU + SEC, FFN_IT - 1, xn)
            for k in range(3):
                for u in range(SEC):
                    at = {2 * i: [(hid_ready, 4 * k + i + 1)] for i in range(4)} if u == 0 else None
                    unit(N_DN + SEC * k + u, u, u % 2, hid, C, 256, x0=C * k, at=at, last_unit=k == 2 and u == SEC - 1)
            ple(0, N_PLE[0])

            mixer(1)
            norm_stats()
            bank = aux_bank()
            for c in range(C):
                if c % 2 == 0:
                    pe.wait_ge(nf_ready, 4 * 4 + c // 2 + 1)
                last = nc.tensor.matmul(bank[0:NE, 0:T], rt[:, c, :], nf[:, c, :], start=(c == 0), stop=(c == C - 1))
            last.then_inc(aux_full, 1)
            bank = aux_bank()
            pe.wait_ge(aux_done, AX_LGT)
            for t, (lo, n) in enumerate(TOK):
                last = nc.tensor.transpose(bank[0:n, t * NE:(t + 1) * NE], lgt[:, lo:lo + n], ident[0:NE, 0:NE])
            last.then_inc(aux_full, 1)

            def rows_of_tokens(s):
                for t, (lo, n) in enumerate(TOK):
                    bank = aux_bank().bitcast(F16)
                    for c in range(C):
                        last = nc.tensor.transpose(bank[0:n, c * P:(c + 1) * P], xn[:, s, c, lo:lo + n], identh[:])
                    last.then_inc(aux_full, 1)

            pe.wait_ge(xn_ready, 4 * 5)
            rows_of_tokens(0)
            keep_warm(8)
            pe.wait_ge(mask_ready, 1)
            bank = aux_bank()
            for t, (lo, n) in enumerate(TOK):
                last = nc.tensor.transpose(bank[0:NE, lo:lo + n], rank[0:n, t, :], ident[0:n, 0:n])
            last.then_inc(aux_full, 1)
            keep_warm(8)
            pe.wait_ge(pos_ready, 1)
            bank = aux_bank()
            for t, (lo, n) in enumerate(TOK):
                nc.tensor.transpose(bank[0:n, t * NE:(t + 1) * NE], cum[:, lo:lo + n], ident[0:NE, 0:NE])
            nc.tensor.matmul(bank[0:1, 3 * NE:3 * NE + 1], over[:], ones[0:NE, 0:1], start=True,
                             stop=True).then_inc(aux_full, 1)
            rows_of_tokens(1)

            pe.wait_ge(aux_done, AX_ROUTED)
            def slots_by_token(bank):
                for t, (lo, n) in enumerate(TOK):
                    last = nc.tensor.transpose(bank.bitcast(F16)[0:CAP, lo:lo + n], sel[0:n, t, :], identh[0:n, 0:n])
                return last

            spilled = pe.value_load(flag[0:1, 0:1], min_val=0, max_val=1)
            with pe.If(spilled > 0):
                with pe.Fori(0, SPILLS) as p:
                    with pe.Fori(0, NE) as e:
                        q = p * NE + e
                        pe.wait_ge(sp_sel, q + 1)
                        pe.wait_ge(sp_h, q * C + 1)
                        for c in range(C):
                            bank = aux[:, c // 4, (c % 4) * CAP:(c % 4 + 1) * CAP]
                            for i in range(6):
                                t, n = i // 2, TOK[i // 2][1]
                                nc.tensor.matmul(bank, nt[0:n, i % 2, t, c * P:(c + 1) * P], sel[0:n, t, :],
                                                 start=(i == 0), stop=(i == 5))
                        for t, (_, n) in enumerate(TOK):
                            last = nc.tensor.matmul(aux[0:CAP, 2, 0:2], sel[0:n, t, :], prs_e[0:n, t, :],
                                                    start=(t == 0), stop=(t == 2))
                        slots_by_token(aux[:, 3, :]).then_inc(sp_gat, 1)
                        with pe.Fori(0, EC) as j:
                            pe.wait_ge(sp_x, q + 1)
                            pe.wait_ge(sp_w, (q * (EC + C) + j) * 32 + 32)
                            pe.wait_ge(sp_gu, q * EC + (j + 1))
                            for g in range(2):
                                for k in range(C):
                                    w = ow[:, g * 1024 + k * P:g * 1024 + (k + 1) * P]
                                    last = nc.tensor.matmul(acc[:, g, 0:CAP], w, xg_f[:, k, :], start=(k == 0),
                                                            stop=(k == C - 1))
                            last.then_inc(sp_used, 1)
                        with pe.Fori(0, C) as j:
                            pe.wait_ge(sp_hid, (q + 1) * EC + 1)
                            pe.wait_ge(sp_w, (q * (EC + C) + j) * 32 + (EC + 1) * 32)
                            for k in range(EC):
                                last = nc.tensor.matmul(acc[0:CAP, 2, 0:P], hid_f[:, k, :], ow[:, k * P:(k + 1) * P],
                                                        start=(k == 0), stop=(k == EC - 1))
                            last.then_inc(sp_used, 1)
                            pe.wait_ge(sp_ye, q * C + (j + 1))
                            pe.wait_ge(sp_h, q * C + (j + 1))
                            nc.tensor.matmul(acc[:, 3, 0:T], y_f[0:CAP, :], sel_f[0:CAP, :], start=True,
                                             stop=True).then_inc(sp_sc, 1)
                pe.wait_ge(sp_h, SPILLS * NE * C + 1)
            with pe.Else():
                pe.nop()

            def gather(adds):
                for g in range(4):
                    pe.wait_ge(sc_done, adds(g + 5))
                    for c in (2 * g, 2 * g + 1):
                        for s in range(2):
                            at = (c % 2 * 2 + s) * CAP
                            for t, (_, n) in enumerate(TOK):
                                last = nc.tensor.matmul(aux[:, g, at:at + CAP], nt[0:n, s, t, c * P:(c + 1) * P],
                                                        sel[0:n, t, :], start=(t == 0), stop=(t == 2))
                    if g == 3:
                        for t, (_, n) in enumerate(TOK):
                            last = nc.tensor.matmul(aux[0:CAP, g, 4 * CAP:4 * CAP + 2], sel[0:n, t, :], prs_e[0:n, t, :],
                                                    start=(t == 0), stop=(t == 2))
                    last.then_inc(gat_full, 1)

            def scatter(chunks, free):
                for c in chunks:
                    if free:
                        free(c)
                    nc.tensor.matmul(aux[:, c % 4, 0:T], ye[0:CAP, 0, c * P:(c + 1) * P], sel_t[0:CAP, :],
                                     start=True, stop=False)
                    nc.tensor.matmul(aux[:, c % 4, 0:T], ye[0:CAP, 1, c * P:(c + 1) * P], sel_t[0:CAP, :],
                                     start=False, stop=True).then_inc(sc_full, 1)

            pe.wait_ge(sel_ready, 1)
            gather(lambda i: i)
            with pe.Fori(0, NE) as e:
                pe.wait_ge(gat_done, e * 4 + 4)
                for u in range(MOE_GU):
                    n = N_MOE + u
                    pe.wait_ge(evac_done, e * MOE_EVAC + (n - 1))
                    pe.wait_ge(hi_done, e * MOE_U + (n + 1))
                    pe.wait_ge(lo_done, e * MOE_U + (n + 1))
                    th = wh[:, u % SLOTS, :].rearrange("p (c m) -> p c m", c=C)
                    tl = wl[:, u % SLOTS, :].rearrange("p (c m) -> p c m", c=C)
                    for m in range(2):
                        bank = acc[:, u % 2, m * CAP:(m + 1) * CAP]
                        for k in range(C):
                            hi, lo = th[:, k, m * P:(m + 1) * P], tl[:, k, m * P:(m + 1) * P]
                            nc.tensor.matmul(bank, hi, xg[:, 0, k, :], start=(k == 0), stop=False)
                            nc.tensor.matmul(bank, hi, xg[:, 1, k, :], start=False, stop=False)
                            last = nc.tensor.matmul(bank, lo, xg[:, 0, k, :], start=False, stop=(k == C - 1))
                    last.then_inc(unit_mm, 1)
                    if u == 1:
                        pe.wait_ge(ys_ready, e * 2 + 2)
                        pe.wait_ge(selt_ready, e + 1)
                        scatter(range(4), None)
                    if u in (4, 6):
                        scatter(range(u, u + 2), lambda i: pe.wait_ge(sc_done, e * 8 + (8 + i - 3)))
                    if u == 7:
                        pe.wait_ge(sc_done, e * 8 + (8 + 5))
                        slots_by_token(aux[:, 0, :]).then_inc(selt_full, 1)
                pe.wait_ge(sel_ready, e + 2)
                gather(lambda i: e * 8 + (i + 8))
                for u in range(MOE_DN):
                    n = N_MOE + MOE_GU + u
                    half, k0 = u // 4, u % 4 * DN_K
                    pe.wait_ge(hi_done, e * MOE_U + (n + 1))
                    pe.wait_ge(lo_done, e * MOE_U + (n + 1))
                    if k0 == 0:
                        pe.wait_ge(ys_ready, e * 2 + (half + 1))
                    th = wh[:, u % SLOTS, 0:DN_K * 512].rearrange("p (c m) -> p c m", c=DN_K)
                    tl = wl[:, u % SLOTS, 0:DN_K * 512].rearrange("p (c m) -> p c m", c=DN_K)
                    for k in range(DN_K):
                        if half == 0 and (k0 + k) % 2 == 0:
                            pe.wait_ge(hid_ready, e * 6 + (FFN_IT * 2 + (k0 + k) // 2 + 1))
                        bank = acc[0:CAP, 2 + half, :]
                        first, end = k0 + k == 0, k0 + k == EC - 1
                        nc.tensor.matmul(bank, hid_e[:, 0, k0 + k, :], th[:, k, :], start=first, stop=False)
                        nc.tensor.matmul(bank, hid_e[:, 0, k0 + k, :], tl[:, k, :], start=False, stop=False)
                        last = nc.tensor.matmul(bank, hid_e[:, 1, k0 + k, :], th[:, k, :], start=False, stop=end)
                    last.then_inc(unit_mm, 1)
            pe.wait_ge(selt_ready, NE + 1)
            pe.wait_ge(gat_done, 4 * NE + 4)
            pe.wait_ge(ys_ready, 2 * NE + 1)
            scatter(range(4), None)
            keep_warm(26)
            pe.wait_ge(ys_ready, 2 * NE + 2)
            scatter(range(4, 8), lambda i: pe.wait_ge(sc_done, 8 + 8 * NE + i - 3))
            keep_warm(2)
            pe.wait_ge(sc_done, 8 * NE + 8 + (4 + ax[0] % 4) + 1)
            ple(1, N_PLE[1])

            norm_stats()
            for g in range(2):
                pe.wait_ge(nf_ready, 4 * 6 + 2 * g + 2)
                for t, (lo, n) in enumerate(TOK):
                    bank = aux_bank()
                    for c in range(4):
                        last = nc.tensor.transpose(bank[0:n, c * P:(c + 1) * P], nf[:, 4 * g + c, lo:lo + n], ident[:])
                    last.then_inc(aux_full, 1)

        @block.scalar
        def _(act):
            ax, ots, prs = [0], [0], [0]

            def aux_bank():
                i = ax[0]
                ax[0] += 1
                act.wait_ge(aux_full, i + 1)
                return aux[:, i % 4, :]

            def hi(n, size=UNIT, it=None, step=0):
                s = n % SLOTS
                from_slot, turn = raw_turn(n)
                extra = 0 if it is None else it * step
                per_turn = 0 if it is None else step // (SLOTS if step == SEC else MOE_SLOTS)
                act.wait_ge(w_loaded[from_slot], 16 * turn if it is None else it * (16 * per_turn) + 16 * turn)
                if n >= SLOTS:
                    act.wait_ge(unit_mm, (n - LEAD) if it is None else extra + (n - LEAD))
                nc.scalar.activation(wh[:, s, 0:size], raw_slot[from_slot][:, 0:size], ACT.Copy, scale=WS).then_inc(hi_done, 1)

            def psum_ready(n, it=None, step=0):
                act.wait_ge(unit_mm, n + 1 if it is None else it * step + (n + 1))
                return acc[:, 2 * (n % 2):2 * (n % 2) + 2, 0:T]

            def tell():
                return act_step, 1

            vec_seen = [0]

            def from_vector():
                vec_seen[0] += 1
                act.wait_ge(vec_step, vec_seen[0])

            def stats():
                nc.scalar.activation(root[:], eps[:], ACT.Sqrt)
                bank = aux_bank()
                nc.scalar.activation(std[:], bank[:, 0:T], ACT.Sqrt, bias=eps[:], scale=1.0 / D)
                nc.scalar.activation(var[:], bank[:, 0:T], ACT.Identity, bias=eps[:], scale=1.0 / D).then_inc(aux_done, 1)

            norm = [0]

            def norm_hi():
                for i in range(C // 2):
                    act.wait_ge(nf_ready, 4 * norm[0] + i + 1)
                    nc.scalar.activation(xn[:, 0, 2 * i:2 * i + 2, :], nf[:, 2 * i:2 * i + 2, :], ACT.Copy,
                                         scale=XS).then_inc(nh_ready, 1)
                norm[0] += 1

            def evac(n, dst, func=ACT.Copy, scale=UNSCALE):
                nc.scalar.activation(dst, psum_ready(n), func, scale=scale).then_inc(evac_done, 1)

            tiles = [0]

            def evac_ot(n, func=ACT.Copy, scale=UNSCALE, last_unit=False):
                if ots[0] >= 2:
                    act.wait_ge(ot_free, ots[0] - 1)
                dst = ot[:, ots[0] % 2]
                ots[0] += 1
                if last_unit:
                    tiles[0] += 1
                    act.wait_ge(tile_mm, tiles[0])
                    nc.scalar.activation(dst[:, 0], acc[:, 2 * (n % 2), 0:T], func, scale=scale).then_inc(tile_out, 1)
                    nc.scalar.activation(dst[:, 1], psum_ready(n)[:, 1], func, scale=scale).then_inc(evac_done, 1)
                else:
                    evac(n, dst, func, scale)

            act.wait_ge(const_ready, N_FIRST)
            for c in range(C):
                nc.scalar.activation(h[:, c, :], aux_bank()[:, 0:T], ACT.Copy).then_inc(aux_done, 1)
            hi(0)

            def small_rows():
                for g in range(2):
                    nc.scalar.activation(vec[:, 4 * g:4 * g + 4, 0:N_ROWS],
                                         aux_bank().rearrange("p (c r) -> p c r", c=4)[:, :, 0:N_ROWS],
                                         ACT.Copy).then_inc(aux_done, 1)

            def embeddings():
                for l in range(LAYERS):
                    for c in range(PC):
                        nc.scalar.activation(pt[:, l, c, :], aux_bank()[:, 0:T], ACT.Copy).then_inc(aux_done, 1)

            def mixer(l):
                n0 = N_MIX[l]
                stats()
                if l == 0:
                    small_rows()
                norm_hi()
                if l == 0:
                    hi(1)
                    hi(2)
                for u in range(SEC):
                    hi(n0 + u + LEAD)
                    evac(n0 + u, xa[:, 2 * u:2 * u + 2, 3:3 + T])
                if l == 0:
                    embeddings()
                n = n0 + SEC
                for u in range(SEC):
                    hi(n + u + LEAD)
                    evac(n + u, ya[:, 2 * u:2 * u + 2, :])
                    if l == 0 and u == 0:
                        from_vector()
                        nc.scalar.activation(lam_b[:], lam_a[:], ACT.Exp, scale=-1.0).then_inc(*tell())
                n += SEC
                for u in range(SEC):
                    hi(n + u + LEAD)
                    evac(n + u, xb[:, 2 * u:2 * u + 2, :])
                    if u == 1:
                        from_vector()
                        nc.scalar.activation(gx, gx, ACT.Tanh).then_inc(*tell())
                from_vector()
                for g, dst in enumerate((gx, gy)):
                    for c in range(C):
                        last = nc.scalar.activation(dst[:, c, :], aux_bank()[:, 0:T], ACT.Tanh, scale=0.5,
                                                    bias=hb[:, c, 2 * g + l:2 * g + l + 1])
                        last.then_inc(aux_done, 1)
                n += SEC
                for u in range(SEC):
                    hi(n + u + LEAD)
                    evac(n + u, ub[:, 2 * u:2 * u + 2, 2:2 + T])
                from_vector()
                nc.scalar.activation(gb_f, gy, ACT.Exp, scale=-1.0)
                nc.scalar.activation(ga_f, gy, ACT.Tanh, bias=tiny[:]).then_inc(*tell())
                n += SEC
                for u in range(SEC):
                    hi(n + u + LEAD)
                    evac_ot(n + u)
                    if u == 2:
                        from_vector()
                        nc.scalar.activation(gy, gy, ACT.Sqrt).then_inc(*tell())
                n += SEC
                for dst in (sa, sg):
                    for u in range(SEC):
                        hi(n + u + LEAD)
                        evac(n + u, dst[:, 2 * u:2 * u + 2, :], ACT.Tanh, 0.5 * UNSCALE)
                    n += SEC
                if l:
                    act.wait_ge(rows_out, 16 * 6 * l)
                for g in range(2):
                    nc.scalar.activation(rows[0:30, g * 512:(g + 1) * 512], aux_bank()[0:30, :],
                                         ACT.Copy).then_inc(aux_done, 1)
                for m in range(3):
                    for u in range(SEC):
                        late = n + u + LEAD >= N_MOE
                        if not late:
                            hi(n + u + LEAD)
                        evac_ot(n + u, last_unit=m == 2 and u == SEC - 1)
                        if late and u < SEC - 1:
                            hi(n + u + LEAD)
                    n += SEC

            def ple(l, n):
                stats()
                for m in range(4):
                    nc.scalar.activation(ya[:, m, :], aux_bank()[:, 0:T], ACT.Copy).then_inc(aux_done, 1)
                norm_hi()
                for m in range(4, C):
                    last = nc.scalar.activation(ya[:, m, :], aux_bank()[:, 0:T], ACT.Copy)
                    last.then_inc(aux_done, 1)
                for u in range(SEC):
                    if n + u + LEAD < N_END:
                        hi(n + u + LEAD)
                    evac_ot(n + u, ACT.Tanh, 0.5 * UNSCALE, last_unit=u == SEC - 1)

            def gate_up(n, u, p, it, step, pairs):
                src = psum_ready(n, it, step)
                s = p % 2
                if u % 2 == 0:
                    act.wait_ge(pair_free, it * pairs + (prs[0] + p + 1))
                    nc.scalar.activation(pair_g[:, s], src, ACT.Copy, scale=UNSCALE)
                    nc.scalar.activation(pair_t[:, s], src, ACT.Tanh, scale=0.5 * UNSCALE).then_inc(evac_done, 1)
                else:
                    nc.scalar.activation(pair_u[:, s], src, ACT.Copy, scale=UNSCALE).then_inc(evac_done, 1)

            mixer(0)
            stats()
            norm_hi()
            with act.Fori(0, FFN_IT) as it:
                for u in range(SEC):
                    hi(N_GU + u + LEAD, it=it, step=SEC)
                    gate_up(N_GU + u, u, u // 2, it, SEC, 2)
            prs[0] += 2 * FFN_IT
            for k in range(3):
                for u in range(SEC):
                    n = N_DN + SEC * k + u
                    hi(n + LEAD)
                    evac_ot(n, last_unit=k == 2 and u == SEC - 1)
            ple(0, N_PLE[0])
            mixer(1)
            stats()
            hi(N_MOE + LEAD - 1)
            norm_hi()
            nc.scalar.activation(lgt[:], aux_bank()[0:NE, 0:T], ACT.Copy).then_inc(aux_done, 1)
            bank = aux_bank()
            nc.scalar.activation(lg[:, 0:2, :], bank[:, 0:2 * NE].rearrange("p (t e) -> p t e", e=NE), ACT.Copy)
            nc.scalar.activation(lg[0:NSAMP, 2, :], bank[0:NSAMP, 2 * NE:3 * NE], ACT.Copy).then_inc(aux_done, 1)

            def rows_of_tokens(s):
                for t, (_, n) in enumerate(TOK):
                    nc.scalar.activation(nt[0:n, s, t, :], aux_bank().bitcast(F16)[0:n, :],
                                         ACT.Copy).then_inc(aux_done, 1)

            rows_of_tokens(0)
            nc.scalar.activation(mask_t, aux_bank()[0:NE, 0:T], ACT.Copy).then_inc(aux_done, 1)
            from_vector()
            nc.scalar.activation(pr[:], pr[:], ACT.Exp).then_inc(*tell())
            bank = aux_bank()
            for t, (_, n) in enumerate(TOK):
                nc.scalar.activation(pos[0:n, t, 0:NE], bank[0:n, t * NE:(t + 1) * NE], ACT.Copy)
            nc.scalar.activation(flag[:], bank[0:1, 3 * NE:3 * NE + 1], ACT.Sign).then_inc(aux_done, 1)
            rows_of_tokens(1)

            act.wait_ge(aux_done, AX_POS)
            spilled = act.value_load(flag[0:1, 0:1], min_val=0, max_val=1)
            with act.If(spilled > 0):
                with act.Fori(0, SPILLS) as p:
                    with act.Fori(0, NE) as e:
                        q = p * NE + e
                        act.wait_ge(sp_gat, q + 1)
                        for g in range(2):
                            nc.scalar.activation(xg_f[:, 4 * g:4 * g + 4, :],
                                                 aux[:, g, 0:4 * CAP].rearrange("p (c t) -> p c t", c=4),
                                                 ACT.Copy, scale=1.0 / XS)
                        nc.scalar.activation(sel_f[0:CAP, :], aux[:, 3, :].bitcast(F16)[0:CAP, 0:T], ACT.Copy)
                        nc.scalar.activation(csr[0:CAP, :], aux[0:CAP, 2, 0:2], ACT.Copy).then_inc(sp_x, 1)
                        with act.Fori(0, EC) as j:
                            act.wait_ge(sp_used, q * (EC + C) + (j + 2))
                            act.wait_ge(sp_hid, q * EC + (j + 1))
                            nc.scalar.activation(pair_g[:, 0, 0, 0:CAP], acc[:, 0, 0:CAP], ACT.Copy)
                            nc.scalar.activation(pair_t[:, 0, 0, 0:CAP], acc[:, 0, 0:CAP], ACT.Tanh, scale=0.5)
                            nc.scalar.activation(pair_u[:, 0, 0, 0:CAP], acc[:, 1, 0:CAP],
                                                 ACT.Copy).then_inc(sp_gu, 1)
                        with act.Fori(0, C) as j:
                            act.wait_ge(sp_csl, q + 1)
                            act.wait_ge(sp_used, q * (EC + C) + (j + (EC + 2)))
                            nc.scalar.activation(y_f[0:CAP, :], acc[0:CAP, 2, 0:P], ACT.Identity,
                                                 scale=csl[0:CAP, :]).then_inc(sp_ye, 1)
                            act.wait_ge(sp_sc, q * C + (j + 1))
            with act.Else():
                act.nop()

            def gathered(fills, seen):
                for g in fills:
                    act.wait_ge(gat_full, seen(g + 1))
                    last = nc.scalar.activation(xg[:, :, 2 * g:2 * g + 2, :].rearrange("p s c t -> p c s t"),
                                                aux[:, g, 0:4 * CAP].rearrange("p (c s t) -> p c s t", c=2, s=2),
                                                ACT.Copy)
                    if g == 3:
                        last = nc.scalar.activation(csr[0:CAP, :], aux[0:CAP, g, 4 * CAP:4 * CAP + 2], ACT.Copy)
                    last.then_inc(gat_done, 1)

            gathered(range(4), lambda i: i)
            with act.Fori(0, NE) as e:
                for u in range(MOE_GU):
                    n = N_MOE + u
                    hi(n + LEAD, moe_unit_size(u + LEAD), e, MOE_U)
                    act.wait_ge(unit_mm, e * MOE_U + (n + 1))
                    src = acc[:, u % 2, 0:2 * CAP].rearrange("p (c t) -> p c t", c=2)
                    k = u // 2 % 2
                    if u % 2 == 0:
                        act.wait_ge(pair_free, e * 6 + (2 * FFN_IT + u // 2 + 1))
                        nc.scalar.activation(pair_g[:, k, :, 0:CAP], src, ACT.Copy, scale=UNSCALE)
                        nc.scalar.activation(pair_t[:, k, :, 0:CAP], src, ACT.Tanh,
                                             scale=0.5 * UNSCALE).then_inc(evac_done, 1)
                    else:
                        nc.scalar.activation(pair_u[:, k, :, 0:CAP], src, ACT.Copy, scale=UNSCALE).then_inc(evac_done, 1)
                    if u == 7:
                        act.wait_ge(selt_full, e + 1)
                        nc.scalar.activation(sel_t[0:CAP, :], aux[:, 0, :].bitcast(F16)[0:CAP, 0:T],
                                             ACT.Copy).then_inc(selt_ready, 1)
                for u in range(MOE_DN):
                    n = N_MOE + MOE_GU + u
                    hi(n + LEAD, moe_unit_size(MOE_GU + u + LEAD), e, MOE_U)
                    if u < 2:
                        gathered((2 * u, 2 * u + 1), lambda i: e * 4 + (i + 4))
                    if u in (4, 7):
                        half = u // 5
                        act.wait_ge(unit_mm, e * MOE_U + (N_MOE + MOE_GU + 4 * half + 4))
                        act.wait_ge(csl_ready, e + 1)
                        act.wait_ge(sc_full, e * 8 + 8)
                        nc.scalar.activation(ye[0:CAP, 0, half * 512:(half + 1) * 512], acc[0:CAP, 2 + half, :],
                                             ACT.Identity, scale=csl[0:CAP, :]).then_inc(evac_done, 1)
            ple(1, N_PLE[1])
            stats()
            for g in range(2):
                for t, (_, n) in enumerate(TOK):
                    nc.scalar.activation(yrows[0:n, t, g * 512:(g + 1) * 512], aux_bank()[0:n, :],
                                         ACT.Copy).then_inc(aux_done, 1)

        @block.vector
        def _(vec_e):
            V = nc.vector
            count = {}
            loop = [None, {}]
            prev = [None]

            def op(ins, s=dv, by=1):
                count[s] = count.get(s, 0) + by
                ins.then_inc(s, by)
                prev[0] = s

            def settle():
                s = prev[0]
                vec_e.wait_ge(s, count[s] if loop[0] is None else loop[0] * loop[1][s] + count[s])

            def lo(n, size=UNIT, it=None, step=0):
                s = n % SLOTS
                vec_e.wait_ge(hi_done, n + 1 if it is None else it * step + (n + 1))
                op(V.scalar_tensor_tensor(out=wl[:, s, 0:size], in0=raw_slot[raw_turn(n)[0]][:, 0:size], scalar=WS,
                                          in1=wh[:, s, 0:size], op0=ALU.mult, op1=ALU.subtract), lo_done)

            def evacuated(n, it=None, step=0):
                n += 1 - (UNCOUNTED if n >= N_PLE[1] else 0)
                vec_e.wait_ge(evac_done, n if it is None else it * step + n)

            act_seen = [0]

            def from_scalar():
                act_seen[0] += 1
                vec_e.wait_ge(act_step, act_seen[0])

            def col(row, c):
                return vec[:, c, row:row + 1]

            def cols(row, n):
                return vec[:, :, row:row + 1].to_broadcast([P, C, n])

            def square(i):
                op(V.tensor_tensor(sq[:, 2 * i:2 * i + 2, :], h[:, 2 * i:2 * i + 2, :], h[:, 2 * i:2 * i + 2, :],
                                   ALU.mult), sq_ready if i == 3 else dv, 2 if i == 3 else 1)
                if i in (1, 2):
                    settle()
                    op(V.tensor_tensor(sq[:, 0:2, :], sq[:, 0:2, :], sq[:, 2 * i:2 * i + 2, :], ALU.add),
                       sq_ready if i == 2 else dv)

            tiles = [0]

            def last_to_h(n, add):
                for i, c in enumerate((C - 2, C - 1)):
                    if i == 0:
                        tiles[0] += 1
                        vec_e.wait_ge(tile_out, tiles[0])
                    else:
                        evacuated(n)
                    add(c, ot[:, ots[0] % 2, i], ot_free if i else dv)
                    settle()
                    op(V.tensor_tensor(sq[:, c, :], h[:, c, :], h[:, c, :], ALU.mult), sq_ready)
                ots[0] += 1

            def plain_add(c, src, sig):
                op(V.tensor_tensor(h[:, c, :], h[:, c, :], src, ALU.add), sig)

            norms = [0]

            def norm(gain, split=True):
                k = norms[0]
                norms[0] += 1
                vec_e.wait_ge(aux_done, AX_NORM[k])
                op(V.reciprocal(rstd[:], std[:]))
                settle()
                op(V.tensor_tensor(rtmp[:], rstd[:], rstd[:], ALU.mult))
                settle()
                op(V.scalar_tensor_tensor(out=rtmp[:], in0=rtmp[:], scalar=-0.5, in1=var[:], op0=ALU.mult, op1=ALU.mult))
                settle()
                op(V.scalar_tensor_tensor(out=rstd[:], in0=rtmp[:], scalar=1.5, in1=rstd[:], op0=ALU.add, op1=ALU.mult))
                settle()

                def low(i):
                    vec_e.wait_ge(nh_ready, 4 * k + i + 1)
                    s = slice(2 * i, 2 * i + 2)
                    op(V.scalar_tensor_tensor(out=xn[:, 1, s, :], in0=nf[:, s, :], scalar=XS, in1=xn[:, 0, s, :],
                                              op0=ALU.mult, op1=ALU.subtract), xn_ready)

                if k == 0:
                    vec_e.wait_ge(aux_done, AX_VEC)
                for i in range(C // 2):
                    for c in (2 * i, 2 * i + 1):
                        op(V.scalar_tensor_tensor(out=nf[:, c, :], in0=h[:, c, :], scalar=col(gain, c), in1=rstd[:],
                                                  op0=ALU.mult, op1=ALU.mult), dv if c % 2 == 0 else nf_ready)
                    if split and i:
                        low(i - 1)
                if split:
                    low(C // 2 - 1)

            def conv(out, src, taps, row, bias, u):
                two = (2 * u, 2 * u + 1)
                for j in range(taps):
                    for c in two:
                        if j == 0 and bias is None:
                            i = V.tensor_scalar(out[:, c, 0:SEQ], src[:, c, 0:SEQ], col(row, c), None, ALU.mult)
                        elif j == 0:
                            i = V.tensor_scalar(out[:, c, 0:SEQ], src[:, c, 0:SEQ], col(row, c), col(bias, c),
                                                ALU.mult, ALU.add)
                        else:
                            i = V.scalar_tensor_tensor(out=out[:, c, 0:SEQ], in0=src[:, c, j:j + SEQ],
                                                       scalar=col(row + j, c), in1=out[:, c, 0:SEQ],
                                                       op0=ALU.mult, op1=ALU.add)
                        op(i)
                    settle()

            def conv_samples(out, src, taps, row, bias, sig=dv):
                old = taps - 1 + T
                for j in range(taps):
                    at = old + NSAMP * j if j < taps - 1 else old - NSAMP
                    dst = smp if j == 0 else smq
                    op(V.tensor_tensor(dst[:], src[:, :, at:at + NSAMP], cols(row + j, NSAMP), ALU.mult))
                    settle()
                    if j:
                        end = j == taps - 1 and bias is None
                        op(V.tensor_tensor(out[:, :, SEQ:T] if end else smp[:], smp[:], smq[:], ALU.add))
                        settle()
                if bias is not None:
                    op(V.tensor_tensor(out[:, :, SEQ:T], smp[:], cols(bias, NSAMP), ALU.add), sig)

            for i in range(C // 2):
                vec_e.wait_ge(aux_done, 2 * i + 2)
                square(i)
            lo(0)

            def softplus():
                r = v("lru_bx")
                op(V.tensor_scalar(hb[:], vec[:, :, r:r + 4], 0.5, None, ALU.mult))
                r = v("lru_lambda")
                lam = vec[:, :, r:r + LAYERS]
                op(V.scalar_tensor_tensor(out=lam_a[:], in0=lam, scalar=-1.0, in1=lam, op0=ALU.mult, op1=ALU.max), vec_step)
                op(V.tensor_scalar(lam_c[:], lam, -4.0, 0.0, ALU.mult, ALU.max))
                from_scalar()
                op(V.tensor_scalar(lam_d[:], lam_b[:], 2.0, None, ALU.add))
                settle()
                op(V.reciprocal(lam_d[:], lam_d[:]))
                settle()
                op(V.tensor_tensor(lam_b[:], lam_b[:], lam_d[:], ALU.mult))
                settle()
                op(V.tensor_tensor(lam_d[:], lam_b[:], lam_b[:], ALU.mult))
                settle()
                op(V.tensor_scalar(lam_a[:], lam_d[:], 1.0 / 15, None, ALU.mult))
                settle()
                for k in (13, 11, 9, 7, 5, 3):
                    op(V.scalar_tensor_tensor(out=lam_a[:], in0=lam_a[:], scalar=1.0 / k, in1=lam_d[:],
                                              op0=ALU.add, op1=ALU.mult))
                    settle()
                op(V.scalar_tensor_tensor(out=lam_a[:], in0=lam_a[:], scalar=1.0, in1=lam_b[:], op0=ALU.add, op1=ALU.mult))
                settle()
                op(V.scalar_tensor_tensor(out=sp4[:], in0=lam_a[:], scalar=8.0, in1=lam_c[:], op0=ALU.mult, op1=ALU.add))

            def mixer(l):
                n0 = N_MIX[l]
                norm(v("norm_mix", l))
                if l == 0:
                    lo(1)
                    lo(2)
                for j in range(3):
                    r = v("state_conv_a") + 24 * l + j
                    op(V.tensor_copy(xa[:, :, 3 + T + NSAMP * j:3 + T + NSAMP * (j + 1)], vec[:, :, r:r + 22:3]))
                for j in range(2):
                    r = v("state_conv_b") + 16 * l + j
                    op(V.tensor_copy(ub[:, :, 2 + T + NSAMP * j:2 + T + NSAMP * (j + 1)], vec[:, :, r:r + 15:2]))
                n = n0
                row, bias = v("conv_a_w", 4 * l), v("conv_a_b", l)
                for u in range(SEC):
                    lo(n + u + LEAD)
                    evacuated(n + u)
                    conv(ua, xa, 4, row, bias, u)
                conv_samples(ua, xa, 4, row, bias, ua_ready)
                if l == 0:
                    vec_e.wait_ge(aux_done, AX_P)
                    softplus()
                n += SEC
                for u in range(SEC):
                    s = slice(2 * u, 2 * u + 2)
                    lo(n + u + LEAD)
                    evacuated(n + u)
                    op(V.tensor_tensor(gx[:, s, :], ya[:, s, :], ya[:, s, :], ALU.mult))
                    settle()
                    op(V.tensor_scalar(gx[:, s, :], gx[:, s, :], 0.044715 * GELU_C, GELU_C, ALU.mult, ALU.add))
                    settle()
                    op(V.tensor_tensor(gx[:, s, :], gx[:, s, :], ya[:, s, :], ALU.mult), vec_step if u == SEC - 1 else dv)
                n += SEC
                for u in range(SEC):
                    lo(n + u + LEAD)
                    if u == 2:
                        from_scalar()
                        op(V.scalar_tensor_tensor(out=ya[:], in0=gx, scalar=1.0, in1=ya[:], op0=ALU.add, op1=ALU.mult),
                           vec_step)
                n += SEC
                row = v("conv_b_w", 3 * l)
                for u in range(SEC):
                    s = slice(2 * u, 2 * u + 2)
                    lo(n + u + LEAD)
                    if u == 0:
                        vec_e.wait_ge(aux_done, AX_GATES[l])
                        for c in range(C):
                            op(V.tensor_scalar(gy[:, c, :], gy[:, c, :], 1.0, sp4[:, c, l:l + 1], ALU.add, ALU.mult),
                               vec_step if c == C - 1 else dv)
                    evacuated(n + u)
                    op(V.tensor_tensor(ub[:, s, 2:2 + T], ub[:, s, 2:2 + T], xb[:, s, :], ALU.mult))
                    settle()
                    conv(xb, ub, 3, row, None, u)
                conv_samples(xb, ub, 3, row, None)
                n += SEC
                for u in range(SEC):
                    s = slice(2 * u, 2 * u + 2)
                    lo(n + u + LEAD)
                    if u == 0:
                        from_scalar()
                        op(V.tensor_tensor(gy, gb_f, gb_f, ALU.mult))
                        settle()
                        op(V.scalar_tensor_tensor(out=gy, in0=gy, scalar=1.0, in1=ga_f, op0=ALU.add, op1=ALU.mult),
                           vec_step)
                    evacuated(n + u)
                    op(V.tensor_tensor(xb[:, s, :], xb[:, s, :], ot[:, ots[0] % 2], ALU.mult), ot_free)
                    ots[0] += 1
                n += SEC
                for u in range(SEC):
                    lo(n + u + LEAD)
                    if u == 0:
                        from_scalar()
                        op(V.scalar_tensor_tensor(out=gx, in0=gx, scalar=1.0, in1=gy, op0=ALU.add, op1=ALU.mult))
                        settle()
                    if u == 1:
                        op(V.scalar_tensor_tensor(out=gx, in0=gx, scalar=0.5, in1=ua, op0=ALU.mult, op1=ALU.mult))
                        settle()
                    if u >= 2:
                        for c in range(4 * (u - 2), 4 * (u - 2) + 4):
                            op(V.tensor_tensor_scan(out=ua[:, c, 0:SEQ], data0=gb_f[:, c, 0:SEQ],
                                                    data1=gx[:, c, 0:SEQ], initial=0.0, op0=ALU.mult, op1=ALU.add))
                r = v("state_lru_h") + NSAMP * l
                op(V.tensor_tensor(smp[:], gb_f[:, :, SEQ:T], vec[:, :, r:r + NSAMP], ALU.mult))
                settle()
                op(V.tensor_tensor(ua[:, :, SEQ:T], smp[:], gx[:, :, SEQ:T], ALU.add))
                settle()
                op(V.tensor_copy(st[:, :, 0:11], xa[:, :, SEQ:SEQ + 11]))
                op(V.tensor_copy(st[:, :, 11:21], ub[:, :, SEQ:SEQ + 10]))
                op(V.tensor_copy(st[:, :, 21:30], ua[:, :, SEQ - 1:T]), st_ready)
                n += SEC
                for u in range(SEC):
                    lo(n + u + LEAD)
                    if u == 0:
                        op(V.scalar_tensor_tensor(out=gx, in0=ya[:], scalar=0.5 * XS, in1=ua, op0=ALU.mult, op1=ALU.mult))
                        settle()
                        op(V.tensor_copy(ga[:, 0], gx))
                        settle()
                    s = slice(2 * u, 2 * u + 2)
                    op(V.tensor_tensor(ga[:, 1, s, :], gx[:, s, :], ga[:, 0, s, :], ALU.subtract), ga_ready)
                op(V.tensor_scalar(gb[:, 0], xb[:], XS, None, ALU.mult))
                settle()
                n += SEC
                for u in range(SEC):
                    s = slice(2 * u, 2 * u + 2)
                    op(V.scalar_tensor_tensor(out=gb[:, 1, s, :], in0=xb[:, s, :], scalar=XS, in1=gb[:, 0, s, :],
                                              op0=ALU.mult, op1=ALU.subtract), gb_ready)
                    lo(n + u + LEAD)
                    evacuated(n + u)
                    op(V.scalar_tensor_tensor(out=ya[:, s, :], in0=sa[:, s, :], scalar=1.0, in1=ot[:, ots[0] % 2],
                                              op0=ALU.add, op1=ALU.mult), ot_free)
                    ots[0] += 1
                n += SEC
                for u in range(SEC):
                    s = slice(2 * u, 2 * u + 2)
                    lo(n + u + LEAD)
                    evacuated(n + u)
                    op(V.scalar_tensor_tensor(out=sg[:, s, :], in0=sg[:, s, :], scalar=1.0, in1=ot[:, ots[0] % 2],
                                              op0=ALU.add, op1=ALU.mult), ot_free)
                    ots[0] += 1
                    settle()
                    last = l == 0 and u == SEC - 1
                    op(V.tensor_tensor(ya[:, s, :], ya[:, s, :], sg[:, s, :], ALU.add),
                       pair_free if last else dv, 2 if last else 1)
                    settle()
                    op(V.tensor_scalar(xn[:, 0, s, :], ya[:, s, :], 0.5 * XS, None, ALU.mult))
                    settle()
                    op(V.scalar_tensor_tensor(out=xn[:, 1, s, :], in0=ya[:, s, :], scalar=0.5 * XS, in1=xn[:, 0, s, :],
                                              op0=ALU.mult, op1=ALU.subtract), xm_ready)
                n += SEC
                for u in range(SEC):
                    late = n + u + LEAD >= N_MOE
                    if not late:
                        lo(n + u + LEAD)
                    if u == SEC - 1:
                        last_to_h(n + u, plain_add)
                    else:
                        evacuated(n + u)
                        add_to_h(u)
                        square(u)
                    if late and u < SEC - 1:
                        lo(n + u + LEAD)

            ots = [0]

            def add_to_h(u):
                s = slice(2 * u, 2 * u + 2)
                op(V.tensor_tensor(h[:, s, :], h[:, s, :], ot[:, ots[0] % 2], ALU.add), ot_free)
                ots[0] += 1
                settle()

            def gated_add(c, src, sig):
                op(V.scalar_tensor_tensor(out=ya[:, c, :], in0=src, scalar=1.0, in1=ya[:, c, :], op0=ALU.add,
                                          op1=ALU.mult), sig)
                settle()
                op(V.scalar_tensor_tensor(out=h[:, c, :], in0=ya[:, c, :], scalar=0.5, in1=h[:, c, :], op0=ALU.mult,
                                          op1=ALU.add))

            def ple(l, n):
                norm(v("norm_ple", l))
                vec_e.wait_ge(aux_done, AX_PLE[l])
                for u in range(SEC):
                    s = slice(2 * u, 2 * u + 2)
                    if n + u + LEAD < N_END:
                        lo(n + u + LEAD)
                    if u == SEC - 1:
                        last_to_h(n + u, gated_add)
                        continue
                    evacuated(n + u)
                    op(V.scalar_tensor_tensor(out=ya[:, s, :], in0=ot[:, ots[0] % 2], scalar=1.0, in1=ya[:, s, :],
                                              op0=ALU.add, op1=ALU.mult), ot_free)
                    ots[0] += 1
                    settle()
                    op(V.scalar_tensor_tensor(out=h[:, s, :], in0=ya[:, s, :], scalar=0.5, in1=h[:, s, :],
                                              op0=ALU.mult, op1=ALU.add))
                    settle()
                    square(u)

            def hidden(p, dst_hi, dst_lo, n=T):
                w, t, g, u = (x[:, p % 2, :, 0:n] for x in (pair_w, pair_t, pair_g, pair_u))
                op(V.scalar_tensor_tensor(out=w, in0=t, scalar=1.0, in1=g, op0=ALU.add, op1=ALU.mult))
                settle()
                op(V.scalar_tensor_tensor(out=w, in0=w, scalar=0.5 * XS, in1=u, op0=ALU.mult, op1=ALU.mult), pair_free)
                settle()
                op(V.tensor_copy(dst_hi, w))
                settle()
                op(V.tensor_tensor(dst_lo, w, dst_hi, ALU.subtract), hid_ready)

            def run_loop(turns, rates, body):
                before = dict(count)
                with vec_e.Fori(0, turns) as it:
                    loop[:] = [it, rates]
                    body(it)
                loop[:] = [None, {}]
                for s, rate in rates.items():
                    assert count[s] - before.get(s, 0) == rate
                    count[s] += rate * (turns - 1)

            mixer(0)
            norm(v("norm_ffn", 0))

            def ffn_turn(it):
                for u in range(SEC):
                    lo(N_GU + u + LEAD, UNIT, it, SEC)
                    if u % 2:
                        evacuated(N_GU + u, it, SEC)
                        at = it * 4 + 2 * (u // 2)
                        hidden(u // 2, hid[:, 0, bass.ds(at, 2), :], hid[:, 1, bass.ds(at, 2), :])

            run_loop(FFN_IT, {lo_done: SEC, dv: 2 * 2, pair_free: 2, hid_ready: 2}, ffn_turn)
            for k in range(3):
                for u in range(SEC):
                    n = N_DN + SEC * k + u
                    lo(n + LEAD)
                    if k == 2 and u == SEC - 1:
                        last_to_h(n, plain_add)
                        continue
                    evacuated(n)
                    add_to_h(u)
                    if k == 2:
                        square(u)
            ple(0, N_PLE[0])
            mixer(1)
            norm(v("norm_ffn", 1))
            lo(N_MOE + LEAD - 1)

            vec_e.wait_ge(aux_done, AX_LOGITS)
            op(V.tensor_reduce(top[:], lg[:], AX.X, ALU.max))
            settle()
            op(V.tensor_tensor(pr[:], lg[:], top[:].unsqueeze(2).to_broadcast([P, 3, NE]), ALU.subtract), vec_step)
            other = lg[:].unsqueeze(2).to_broadcast([P, 3, NE, NE])
            mine = lg[:].unsqueeze(3).to_broadcast([P, 3, NE, NE])
            op(V.tensor_tensor(cmp_b, other, mine, ALU.is_equal))
            op(V.tensor_tensor(cmp_a, other, mine, ALU.is_gt))
            settle()
            op(V.tensor_tensor(cmp_b, cmp_b, tri[:].unsqueeze(1).to_broadcast([P, 3, NE, NE]), ALU.mult))
            settle()
            op(V.tensor_tensor(cmp_a, cmp_a, cmp_b, ALU.add))
            settle()
            op(V.tensor_reduce(rank[:], cmp_a, AX.X, ALU.add))
            settle()
            op(V.tensor_scalar(rank[:], rank[:], 1.5, None, ALU.is_lt), mask_ready)
            settle()
            vec_e.wait_ge(aux_done, AX_MASK)
            op(V.tensor_tensor_scan(out=cum, data0=mask_t, data1=mask_t, initial=0.0, op0=ALU.add, op1=ALU.max))
            settle()
            op(V.tensor_scalar(over[:], cum[:, T - 1:T], float(CAP), None, ALU.is_gt))
            settle()
            op(V.tensor_tensor(cum, cum, mask_t, ALU.mult))
            settle()
            op(V.tensor_scalar(cum, cum, -1.0, None, ALU.add), pos_ready)

            from_scalar()
            op(V.tensor_tensor(pr[:], pr[:], rank[:], ALU.mult))
            settle()
            op(V.tensor_reduce(den[:], pr[:], AX.X, ALU.add))
            settle()
            op(V.reciprocal(den[:], den[:]))
            settle()
            op(V.tensor_tensor(pr[:], pr[:], den[:].unsqueeze(2).to_broadcast([P, 3, NE]), ALU.mult))
            settle()
            op(V.tensor_scalar(prs[:, :, 0:NE, 0], pr[:], XS, None, ALU.mult))
            settle()
            op(V.scalar_tensor_tensor(out=prs[:, :, 0:NE, 1], in0=pr[:], scalar=XS, in1=prs[:, :, 0:NE, 0],
                                      op0=ALU.mult, op1=ALU.subtract))
            op(V.memset(ye[0:CAP], 0.0), ys_ready, 2)
            op(V.memset(sel_t[0:CAP, :], 0.0), selt_ready)
            settle()

            def one_hot(e, sig):
                for t in range(3):
                    op(V.tensor_scalar(sel[:, t, :], iota[:], pos[:, t, bass.ds(e, 1)], None, ALU.is_equal))
                op(V.tensor_copy(prs_e[:], prs[:, :, bass.ds(e, 1), :].rearrange("p t e s -> p t (e s)")), sig)

            vec_e.wait_ge(aux_done, AX_POS)
            spilled = vec_e.value_load(flag[0:1, 0:1], min_val=0, max_val=1)
            with vec_e.If(spilled > 0):
                for i, s in enumerate((sp_gu, sp_hid, sp_h, sp_used)):
                    V.memset(spare[:, i:i + 1], 0.0).then_inc(s, 1)
                with vec_e.Fori(0, SPILLS) as p:
                    V.tensor_scalar(pos[:], pos[:], -float(CAP), None, ALU.add).then_inc(sp_pass, 1)
                    with vec_e.Fori(0, NE) as e:
                        q = p * NE + e
                        vec_e.wait_ge(sp_pass, p + 1)
                        for t in range(3):
                            V.tensor_scalar(sel[:, t, :], iota[:], pos[:, t, bass.ds(e, 1)], None, ALU.is_equal)
                        V.tensor_copy(prs_e[:], prs[:, :, bass.ds(e, 1), :].rearrange("p t e s -> p t (e s)")
                                      ).then_inc(sp_sel, 1)
                        vec_e.wait_ge(sp_x, q + 1)
                        V.scalar_tensor_tensor(out=csl[0:CAP, :], in0=csr[0:CAP, 0:1], scalar=1.0, in1=csr[0:CAP, 1:2],
                                               op0=ALU.mult, op1=ALU.add).then_inc(sp_csl, 1)
                        with vec_e.Fori(0, EC) as j:
                            vec_e.wait_ge(sp_gu, q * EC + (j + 2))
                            V.scalar_tensor_tensor(out=pair_w[:, 0, 0, 0:CAP], in0=pair_t[:, 0, 0, 0:CAP], scalar=1.0,
                                                   in1=pair_g[:, 0, 0, 0:CAP], op0=ALU.add,
                                                   op1=ALU.mult).then_inc(sp_mm, 1)
                            vec_e.wait_ge(sp_mm, q * EC + (j + 1))
                            dst = hid_f[:, bass.ds(j, 1), :].rearrange("p c t -> p (c t)")
                            V.scalar_tensor_tensor(out=dst, in0=pair_w[:, 0, 0, 0:CAP], scalar=0.5,
                                                   in1=pair_u[:, 0, 0, 0:CAP], op0=ALU.mult,
                                                   op1=ALU.mult).then_inc(sp_hid, 1)
                        with vec_e.Fori(0, C) as j:
                            vec_e.wait_ge(sp_sc, q * C + (j + 1))
                            hc = h[:, bass.ds(j, 1), :].rearrange("p c t -> p (c t)")
                            V.scalar_tensor_tensor(out=hc, in0=acc[:, 3, 0:T], scalar=1.0 / XS, in1=hc,
                                                   op0=ALU.mult, op1=ALU.add).then_inc(sp_h, 1)
                V.tensor_scalar(pos[:], pos[:], float(CAP * SPILLS), None, ALU.add).then_inc(sp_pass, 1)
                vec_e.wait_ge(sp_pass, SPILLS + 1)
            with vec_e.Else():
                vec_e.nop()

            def slot_weights():
                op(V.tensor_tensor(csl[0:CAP, :], csr[0:CAP, 0:1], csr[0:CAP, 1:2], ALU.add))
                settle()
                op(V.tensor_scalar(csl[0:CAP, :], csl[0:CAP, :], UNSCALE, None, ALU.mult), csl_ready)

            def add_scattered(c, seen):
                vec_e.wait_ge(sc_full, seen(c + 1))
                op(V.scalar_tensor_tensor(out=h[:, c, :], in0=aux[:, c % 4, 0:T], scalar=1.0 / XS, in1=h[:, c, :],
                                          op0=ALU.mult, op1=ALU.add), sc_done)

            op(V.memset(spare[:, 4:5], 0.0), sc_done, 8)
            one_hot(0, sel_ready)
            vec_e.wait_ge(gat_done, 4)
            slot_weights()

            def expert(e):
                for u in range(MOE_U):
                    n = N_MOE + u
                    lo(n + LEAD, moe_unit_size(u + LEAD), e, MOE_U)
                    if u in (2, 3, 5, 7):
                        c = 2 * (2, 3, 5, 7).index(u)
                        add_scattered(c, lambda i: e * 8 + i)
                        add_scattered(c + 1, lambda i: e * 8 + i)
                    if u == 9:
                        vec_e.wait_ge(selt_full, e + 1)
                        one_hot(e + 1, sel_ready)
                    if u < MOE_GU and u % 2:
                        p = u // 2
                        vec_e.wait_ge(evac_done, e * MOE_EVAC + (n + 1))
                        hidden(p, hid_e[:, 0, 2 * p:2 * p + 2, :], hid_e[:, 1, 2 * p:2 * p + 2, :], CAP)
                    if u in (MOE_GU + 5, MOE_U - 1):
                        half = (u - MOE_GU) // 6
                        vec_e.wait_ge(evac_done, e * MOE_EVAC + (N_MOE + MOE_GU + half + 1))
                        s = slice(half * 512, (half + 1) * 512)
                        op(V.scalar_tensor_tensor(out=ye[0:CAP, 1, s], in0=acc[0:CAP, 2 + half, :],
                                                  scalar=csl[0:CAP, :], in1=ye[0:CAP, 0, s],
                                                  op0=ALU.mult, op1=ALU.subtract), ys_ready)
                settle()
                vec_e.wait_ge(gat_done, e * 4 + 8)
                slot_weights()

            run_loop(NE, {lo_done: MOE_U, dv: 2 * 6 + 3 + 1, pair_free: 6, hid_ready: 6, ys_ready: 2, sc_done: 8,
                          sel_ready: 1, csl_ready: 1}, expert)
            for c in range(C):
                add_scattered(c, lambda i: NE * 8 + i)
                if c % 2:
                    settle()
                    square(c // 2)
            ple(1, N_PLE[1])
            norm(v("final_norm"), split=False)


_INS = ["x_prompt", "x_sample", "state_lru_h", "state_conv_a", "state_conv_b", "p_prompt", "p_sample", "norm_mix",
        "w_in", "conv_a_w", "conv_a_b", "lru_wx", "lru_bx", "lru_wa", "lru_ba", "lru_lambda", "w_a_out", "conv_b_w",
        "w_b_out", "w_o", "norm_ffn", "ffn_w_gu", "ffn_w_dn", "router", "moe_w_gu", "moe_w_dn", "norm_ple",
        "w_ple_gate", "w_ple_proj", "final_norm"]
_OUTS = [("y_prompt", (1, SEQ, D)), ("y_sample", (NSAMP, 1, D)), ("lru_h_prompt", (LAYERS, 1, D)),
         ("conv_a_prompt", (LAYERS, 1, 3, D)), ("conv_b_prompt", (LAYERS, 1, 2, D)),
         ("lru_h_sample", (LAYERS, NSAMP, D)), ("conv_a_sample", (LAYERS, NSAMP, 3, D)),
         ("conv_b_sample", (LAYERS, NSAMP, 2, D))]


def kernel(**inputs):
    import numpy as np
    import concourse.bacc as bacc
    from concourse.bass_utils import run_bass_kernel_spmd

    nc = bacc.Bacc("TRN2", target_bir_lowering=False, num_devices=1)
    arrays, ins, outs = {}, {}, {}
    for name in _INS:
        x = np.ascontiguousarray(inputs[name])
        arrays[f"in_{name}"] = x
        ins[name] = nc.dram_tensor(f"in_{name}", x.shape, mybir.dt.from_np(x.dtype), kind="ExternalInput").ap()
    for name, shape in _OUTS:
        outs[name] = nc.dram_tensor(f"out_{name}", shape, F32, kind="ExternalOutput").ap()
    program(nc, ins, outs)
    r = run_bass_kernel_spmd(nc, [arrays], core_ids=[0])
    return tuple(r.results[0][f"out_{name}"] for name, _ in _OUTS)
```
